# Optimizing a Trainium2 kernel written in Bass

```python
import math
import jax, jax.numpy as jnp
from jax import lax
import numpy as np

D_MODEL = 1024
BATCH = 1
SEQ = 512
DEPTH = 2
DEC_BATCH = 8
DEC_SEQ = 8
PAST_LEN = 512
PAGE_SIZE = 128

N_A_LAYERS = DEPTH // 2
N_B_LAYERS = DEPTH - N_A_LAYERS
HGRN_EXPAND = 128
H_A = D_MODEL // HGRN_EXPAND
DK_A = HGRN_EXPAND
DV_A = D_MODEL // H_A
CHUNK_A = 64
H_B = 16
HD_B = D_MODEL // H_B
Q_BLOCK = 128
D_FF = 4 * D_MODEL
EPS = 1e-6
SB_BIAS_INIT = -6.0

kernel_name = 'yoco_hgrn2_stickbreaking_decoder_step'

def rmsnorm(x, g):
    xf = x.astype(jnp.float32)
    y = xf * lax.rsqrt(jnp.mean(xf * xf, axis=-1, keepdims=True) + EPS) * g.astype(jnp.float32)
    return y.astype(x.dtype)

def sq_relu_mlp(xn, w_up, w_down):
    h = jax.nn.relu(xn @ w_up)
    return (h * h) @ w_down

def hgrn2_mixer(xn, w_in, lb, g_onorm, w_out, S0):
    f32 = jnp.float32
    B, L, _ = xn.shape
    proj = xn @ w_in
    q, fz, iv, og = jnp.split(proj, 4, axis=-1)
    q = jax.nn.silu(q.astype(f32)).reshape(B, L, H_A, DK_A)
    fz = fz.astype(f32).reshape(B, L, H_A, DK_A)
    lb = lb.astype(f32).reshape(H_A, DK_A)
    log_f = jnp.logaddexp(jnp.log(lb), jnp.log1p(-lb) + jax.nn.log_sigmoid(fz))
    k = (1.0 - lb) * jax.nn.sigmoid(-fz)
    v = iv.astype(f32).reshape(B, L, H_A, DV_A)
    C = math.gcd(L, CHUNK_A)
    N = L // C

    def to_chunks(a):
        return jnp.moveaxis(a.reshape(B, N, C, *a.shape[2:]), 1, 0)

    causal = jnp.tril(jnp.ones((C, C), dtype=bool))[None, :, :, None, None]

    def step(S, inp):
        qc, kc, vc, lfc = inp
        G = jnp.cumsum(lfc, axis=1)
        o_inter = jnp.einsum('bthk,bhkv->bthv', qc * jnp.exp(G), S)
        diff = G[:, :, None] - G[:, None, :]
        decay = jnp.exp(jnp.where(causal, diff, -jnp.inf))
        scores = jnp.einsum('bthk,bshk,btshk->bhts', qc, kc, decay)
        o_intra = jnp.einsum('bhts,bshv->bthv', scores, vc)
        G_last = G[:, -1]
        S_new = jnp.exp(G_last)[..., None] * S + jnp.einsum(
            'bshk,bshv->bhkv', kc * jnp.exp(G_last[:, None] - G), vc)
        return S_new, o_inter + o_intra

    S_fin, o = lax.scan(step, S0.astype(f32),
                        (to_chunks(q), to_chunks(k), to_chunks(v), to_chunks(log_f)))
    o = jnp.moveaxis(o, 0, 1).reshape(B, L, H_A, DV_A)
    o = o * lax.rsqrt(jnp.mean(o * o, axis=-1, keepdims=True) + EPS)
    o = o.reshape(B, L, D_MODEL) * g_onorm.astype(f32) * jax.nn.silu(og.astype(f32))
    return o.astype(xn.dtype) @ w_out, S_fin

def stick_breaking(q, k, v, bias, q_offset):
    f32 = jnp.float32
    Lq, Lk = q.shape[1], k.shape[1]
    z = jnp.einsum('bqhd,bkhd->bhqk', q.astype(f32), k.astype(f32)) * (HD_B ** -0.5)
    z = z + bias.astype(f32)[None, :, None, None]
    mask = jnp.arange(Lk)[None, :] < (q_offset + jnp.arange(Lq))[:, None]
    u = jnp.where(mask, jax.nn.log_sigmoid(-z), 0.0)
    rev_excl = lax.cumsum(u, axis=3, reverse=True) - u
    A = jnp.where(mask, jnp.exp(jax.nn.log_sigmoid(z) + rev_excl), 0.0)
    return jnp.einsum('bhqk,bkhd->bqhd', A, v.astype(f32))

def stick_breaking_blocked(q, k_all, v_all, bias, past_len):
    L = q.shape[1]
    qb = math.gcd(L, Q_BLOCK)
    outs = []
    for i in range(L // qb):
        e = past_len + (i + 1) * qb
        outs.append(stick_breaking(q[:, i * qb:(i + 1) * qb], k_all[:, :e], v_all[:, :e],
                                   bias, past_len + i * qb))
    return jnp.concatenate(outs, axis=1)

def run_trunk(x, S0s, past_k, past_v, lb_all, w_in_a, g_onorm_a, w_out_a, w_kv, g_kv,
              w_q_b, w_out_b, sb_bias, w_up, w_down, g_mix, g_mlp, g_final):
    B, L, _ = x.shape
    past_len = past_k.shape[1]
    h = x
    new_S = []
    k_new = None
    v_new = None
    k_all = None
    v_all = None
    for l in range(DEPTH):
        if l < N_A_LAYERS:
            y, S = hgrn2_mixer(rmsnorm(h, g_mix[l]), w_in_a[l], lb_all[l], g_onorm_a[l],
                               w_out_a[l], S0s[l])
            new_S.append(S)
            h = h + y
        else:
            if l == N_A_LAYERS:
                kv = rmsnorm(h, g_kv) @ w_kv
                k_new, v_new = jnp.split(kv, 2, axis=-1)
                k_new = k_new.reshape(B, L, H_B, HD_B)
                v_new = v_new.reshape(B, L, H_B, HD_B)
                k_all = jnp.concatenate([past_k.astype(k_new.dtype), k_new], axis=1)
                v_all = jnp.concatenate([past_v.astype(v_new.dtype), v_new], axis=1)
            j = l - N_A_LAYERS
            q = (rmsnorm(h, g_mix[l]) @ w_q_b[j]).reshape(B, L, H_B, HD_B)
            o = stick_breaking_blocked(q, k_all, v_all, sb_bias[j], past_len)
            h = h + o.reshape(B, L, D_MODEL).astype(h.dtype) @ w_out_b[j]
        h = h + sq_relu_mlp(rmsnorm(h, g_mlp[l]), w_up[l], w_down[l])
    return rmsnorm(h, g_final), jnp.stack(new_S), k_new, v_new

def setup_inputs(seed: int = 0) -> dict:
    key = jax.random.key(seed)
    ks = jax.random.split(key, 24)
    f32 = jnp.float32
    n_pages = PAST_LEN // PAGE_SIZE
    n_used = DEC_BATCH * n_pages
    n_pool = n_used + max(n_used // 4, 1)
    nrm = jax.random.normal
    page_table = jax.random.permutation(ks[0], n_pool)[:n_used].reshape(DEC_BATCH, n_pages).astype(jnp.int32)
    return {
        'x_prompt': nrm(ks[1], (BATCH, SEQ, D_MODEL), f32),
        'x_sample': nrm(ks[2], (DEC_BATCH, DEC_SEQ, D_MODEL), f32),
        'state_hgrn': 0.5 * nrm(ks[3], (N_A_LAYERS, DEC_BATCH, H_A, DK_A, DV_A), f32),
        'cache_k': nrm(ks[4], (n_pool, PAGE_SIZE, H_B, HD_B), f32),
        'cache_v': nrm(ks[5], (n_pool, PAGE_SIZE, H_B, HD_B), f32),
        'page_table': page_table,
        'lb_logits': 0.5 * nrm(ks[6], (N_A_LAYERS + 1, D_MODEL), f32),
        'w_in_a': nrm(ks[7], (N_A_LAYERS, D_MODEL, 4 * D_MODEL), f32) * D_MODEL ** -0.5,
        'g_onorm_a': 1.0 + 0.02 * nrm(ks[8], (N_A_LAYERS, D_MODEL), f32),
        'w_out_a': nrm(ks[9], (N_A_LAYERS, D_MODEL, D_MODEL), f32) * D_MODEL ** -0.5,
        'w_kv': nrm(ks[10], (D_MODEL, 2 * D_MODEL), f32) * D_MODEL ** -0.5,
        'g_kv': 1.0 + 0.02 * nrm(ks[11], (D_MODEL,), f32),
        'w_q_b': nrm(ks[12], (N_B_LAYERS, D_MODEL, D_MODEL), f32) * D_MODEL ** -0.5,
        'w_out_b': nrm(ks[13], (N_B_LAYERS, D_MODEL, D_MODEL), f32) * D_MODEL ** -0.5,
        'sb_bias': SB_BIAS_INIT + 0.1 * nrm(ks[19], (N_B_LAYERS, H_B), f32),
        'w_up': nrm(ks[14], (DEPTH, D_MODEL, D_FF), f32) * D_MODEL ** -0.5,
        'w_down': nrm(ks[15], (DEPTH, D_FF, D_MODEL), f32) * D_FF ** -0.5,
        'g_mix': 1.0 + 0.02 * nrm(ks[16], (DEPTH, D_MODEL), f32),
        'g_mlp': 1.0 + 0.02 * nrm(ks[17], (DEPTH, D_MODEL), f32),
        'g_final': 1.0 + 0.02 * nrm(ks[18], (D_MODEL,), f32),
    }

def reference(x_prompt, x_sample, state_hgrn, cache_k, cache_v, page_table, lb_logits, w_in_a,
              g_onorm_a, w_out_a, w_kv, g_kv, w_q_b, w_out_b, sb_bias, w_up, w_down, g_mix,
              g_mlp, g_final):
    lb_all = jnp.cumsum(jax.nn.softmax(lb_logits.astype(jnp.float32), axis=0), axis=0)
    weights = (lb_all, w_in_a, g_onorm_a, w_out_a, w_kv, g_kv, w_q_b, w_out_b, sb_bias,
               w_up, w_down, g_mix, g_mlp, g_final)
    Bp = x_prompt.shape[0]
    S0_prompt = jnp.zeros((N_A_LAYERS, Bp, H_A, DK_A, DV_A), jnp.float32)
    empty = jnp.zeros((Bp, 0, H_B, HD_B), x_prompt.dtype)
    y_prompt, state_hgrn_prompt, k_prompt, v_prompt = run_trunk(
        x_prompt, S0_prompt, empty, empty, *weights)
    Bs = page_table.shape[0]
    past_k = cache_k[page_table].reshape(Bs, -1, H_B, HD_B)
    past_v = cache_v[page_table].reshape(Bs, -1, H_B, HD_B)
    y_sample, state_hgrn_sample, k_sample, v_sample = run_trunk(
        x_sample, state_hgrn, past_k, past_v, *weights)
    return (y_prompt, y_sample, state_hgrn_prompt, state_hgrn_sample,
            k_prompt, v_prompt, k_sample, v_sample)


_drawn_inputs = setup_inputs


def setup_inputs(seed=0):
    import zlib

    import numpy as np

    out = dict(_drawn_inputs(seed))
    spreads = {}
    factors = {'g_onorm_a': 15.601,
     'g_kv': 21.85,
     'sb_bias': 64.0,
     'g_final': 24.414,
     'g_mlp': 4.853,
     'w_q_b': 8.0,
     'w_out_b': 8.0}
    for name, (base, spread) in spreads.items():
        noise = np.random.default_rng([zlib.crc32(name.encode()), seed]).standard_normal(out[name].shape)
        drawn = base * np.exp(spread * noise) if base else spread * noise
        out[name] = __import__('jax').numpy.asarray(drawn.astype(out[name].dtype))
    for name, factor in factors.items():
        out[name] = (out[name] * factor).astype(out[name].dtype)
    return out
```

```python
from contextlib import ExitStack

import concourse.bass as bass
from concourse import mybir
from concourse.alu_op_type import AluOpType as ALU

ACT = mybir.ActivationFunctionType
F32 = mybir.dt.float32
F32R = mybir.dt.float32r
U32 = mybir.dt.uint32
I32 = mybir.dt.int32

P = 128
DM = 1024
NB = DM // P
SEQ = 512
NSEQ = 8
NEW = 8
SMP = NSEQ * NEW
T = SEQ + SMP
HALF = T // 2
CH = 128
NCH = SEQ // CH
H_B = 16
HD = DM // H_B
NPAIR = H_B // 2
PAGE = 128
NPG = 4
FCH = 4
EPS = 1e-6
CLAMP = -43.0
NEG = -1e30
SCALE = HD ** -0.5
LEVELS = [64, 32, 16, 8, 4, 2, 1]
SMP_LEVELS = 3

LB0, LB1, GON, GKV, GMIX0, GMIX1, GMLP0, GMLP1, GFIN = range(0, 72, 8)


class Count:

    def __init__(self, sem, base=0, i=0, per=0):
        self.sem, self.base, self.i, self.per, self.k = sem, base, i, per, 0

    def inc(self, ins):
        ins.then_inc(self.sem, 1)
        self.k += 1
        return self.at(self.k)

    def at(self, k):
        return self.base + self.i * self.per + k if self.per else self.base + k

    def end(self):
        assert self.k == self.per, (self.k, self.per)


def yoco_step(nc, x_prompt, x_sample, state_hgrn, cache_k, cache_v, page_table, lb_logits, w_in_a,
              g_onorm_a, w_out_a, w_kv, g_kv, w_q_b, w_out_b, sb_bias, w_up, w_down, g_mix, g_mlp,
              g_final, y_prompt, y_sample, st_prompt, st_sample, k_prompt, v_prompt, k_sample, v_sample):
    ctx = ExitStack()
    with ctx:
        top = [nc.sbuf_base + (-nc.sbuf_base) % 64]
        limit = nc.sbuf_usable_end

        def sb_at(name, shape, dt, offset):
            n = 4
            for d in shape[1:]:
                n *= d
            assert offset + n <= limit, (name, offset + n, limit)
            return nc.alloc_sbuf_tensor_at(name, shape, dt, offset=offset), offset + (n + 63) // 64 * 64

        def sb(name, shape, dt=F32):
            t, top[0] = sb_at(name, shape, dt, top[0])
            return t

        def arena(start, items):
            out = []
            for name, shape, dt in items:
                t, start = sb_at(name, shape, dt, start)
                out.append(t)
            return out

        ident = sb("ident", [P, P])
        ones = sb("ones", [P, P])
        ones_r = sb("ones_r", [P, P], F32R)
        tri_r = sb("tri_r", [P, P], F32R)
        ident_r = sb("ident_r", [P, P], F32R)
        gT = sb("gT", [P, 72])
        lb = sb("lb", [P, NB])
        omlb = sb("omlb", [P, NB])
        bias_h = sb("bias_h", [P, H_B])
        eps_t = sb("eps_t", [P, 1])
        small = sb("small", [P, 4 * NB])
        wait_mark = sb("wait_mark", [1, 16])
        start_mark = sb("start_mark", [1, 16])
        neg_r = sb("neg_r", [P, P], F32R)
        neg_s = sb("neg_s", [SMP, SMP])
        pt = sb("pt", [1, NSEQ * NPG], I32)
        rstd = sb("rstd", [P, T])
        hT = sb("hT", [P, NB, T])
        wraw = [sb(f"wraw{s}", [P, 8, 256]) for s in range(2)]
        whi = [sb(f"whi{s}", [P, 8, 256], F32R) for s in range(2)]
        wlo = [sb(f"wlo{s}", [P, 8, 256], F32R) for s in range(2)]
        xa_at = top[0]
        xa_hi = sb("xa_hi", [P, NB, T], F32R)
        xa_lo = sb("xa_lo", [P, NB, T], F32R)
        xb_at = top[0]
        xb_hi = sb("xb_hi", [P, NB, T], F32R)
        xb_lo = sb("xb_lo", [P, NB, T], F32R)
        ar = top[0]


        tri_f, neg_f = arena(xb_at + NB * T * 4 + T * 4, [("tri_f", [P, P], F32), ("neg_f", [P, P], F32)])
        xc_at = xb_at + NB * T * 4
        xe_at = xa_at + NB * T * 4
        hgrn_o = sb_at("hgrn_o", [P, NB, T], F32, xb_at)[0]
        attn_o = sb_at("attn_o", [P, NB, T], F32, xa_at)[0]
        x_rows, xs_rows = arena(xb_at, [("x_rows", [P, SEQ // P, DM], F32), ("xs_rows", [SMP, DM], F32)])
        vec_rows, bias_row = arena(xa_at, [("vec_rows", [72, P], F32), ("bias_row", [1, H_B], F32)])
        TW = [SEQ] * (len(LEVELS) - SMP_LEVELS) + [T] * SMP_LEVELS
        masks, scan_keep, seqmask = arena(ar, [("masks", [P, len(LEVELS), P], F32), ("scan_keep", [P, T], F32),
                                               ("seqmask", [SMP, NSEQ], F32)])
        ar1 = ar + 4 * (len(LEVELS) * P + T) + 64
        (cl0, qq, t1, t2, fg, kk, G, tq, sgg, vT, eG, ek, kh, qe, dg, S, Amat, As, VK, *X) = arena(
            ar1, [(n, [P, T], F32) for n in ["cl0", "qq", "t1", "t2", "fg", "kk", "G", "tq", "sgg", "vT", "eG", "ek",
                                             "kh", "qe", "dg"]]
            + [("S", [P, NCH, P], F32), ("Amat", [P, NCH, P], F32), ("As", [SMP, SMP], F32), ("VK", [P, 2, 5, P], F32)]
            + [(f"X{n}", [P, w], F32) for n, w in enumerate(TW[:-1])])
        D0, D1, S0, Sn, X_last = arena(xc_at, [("D0", [P, T], F32), ("D1", [P, T], F32), ("S0", [P, NSEQ, P], F32),
                                               ("Sn", [P, NSEQ, P], F32), ("X_last", [P, T], F32)])
        X.append(X_last)
        D = [D0, D1]
        (Vblk,) = arena(ar1 + 15 * T * 4 + 2 * 2048 + 256 + 5120, [("Vblk", [SMP, NSEQ, P], F32)])
        GROUPS = [[(3, 0), (2, 128)], [(1, 0)], [(0, 0)]]
        GCOL, GW = [0, 384, 768], [384, 384, 512]
        UOFF = {3: 0, 2: 128, 1: 384, 0: 768}
        qT_at = (limit - NB * T * 4) // 64 * 64
        (qT,) = arena(qT_at, [("qT", [P, NB, T], F32)])
        (kf, vf, khi, klo, qhi, qlo, kr, vr, uh0, ul0, Am, zb0, zb1, tl0, tl1, ul1) = arena(
            ar, [("kf", [P, T], F32), ("vf", [P, T], F32), ("khi", [P, T], F32R), ("klo", [P, T], F32R),
                 ("qhi", [P, SEQ], F32R), ("qlo", [P, SEQ], F32R), ("kr", [P, NCH, P], F32), ("vr", [P, NCH, P], F32),
                 ("uh0", [P, 1280], F32R), ("ul0", [P, 1280], F32R), ("Am", [P, 1280], F32), ("zb0", [P, 512], F32),
                 ("zb1", [P, 512], F32), ("tl0", [P, 512], F32), ("tl1", [P, 512], F32), ("ul1", [P, 1280], F32R)])
        kTs, kvn, uh1 = arena(xe_at, [("kTs", [P, NPAIR, SMP], F32), ("kvn", [SMP, 2, NPAIR, P], F32),
                                      ("uh1", [P, 1280], F32R)])
        uh, ul, zb, tl = [uh0, uh1], [ul0, ul1], [zb0, zb1], [tl0, tl1]
        uhN, ulN = arena(xe_at + 2048 + 8192, [("uhN", [SMP, H_B, SMP], F32R), ("ulN", [SMP, H_B, SMP], F32R)])
        (AN,) = arena(xe_at + 2048, [("AN", [SMP, H_B, SMP], F32)])
        Kp0, Kp1 = arena(xb_at, [(f"Kp{n}", [P, NPG, DM], F32) for n in range(2)])
        (qblk, zbS, tlS, uhS, ulS, AS, biasQ, Vp0, Vp1, KT) = arena(
            ar, [("qblk", [P, NPAIR, NSEQ, 2 * NEW], F32), ("zbS", [P, 512], F32), ("tlS", [P, 512], F32),
                 ("uhS", [P, 512], F32R), ("ulS", [P, 512], F32R), ("AS", [P, 512], F32), ("biasQ", [P, P], F32),
                 ("Vp0", [P, NPG, DM], F32), ("Vp1", [P, NPG, DM], F32), ("KT", [P, NPAIR, NPG, P], F32)])
        Kp, Vp = [Kp0, Kp1], [Vp0, Vp1]
        zbN, tlN, biasN = arena(ar + 14848, [("zbN", [SMP, H_B, SMP], F32), ("tlN", [SMP, H_B, SMP], F32),
                                             ("biasN", [SMP, H_B, SMP], F32)])
        yrow0, yrow1 = arena(xb_at, [("yrow0", [P, DM], F32), ("yrow1", [P, DM], F32)])
        yrow = [yrow0, yrow1]
        nrm, *mlp_t = arena(ar1, [("nrm", [P, NB, T], F32)] + [(f"mlp{i}", [P, T], F32) for i in range(4)])
        relu_t, sqr_t = mlp_t[:2], mlp_t[2:]

        def ps(name, shape):
            return ctx.enter_context(nc.psum_tensor(name, shape, F32))

        acc = [ps(f"acc{s}", [P, 2, 512]) for s in range(2)]
        pL = ps("pL", [P, 2, 512])
        pM = ps("pM", [P, 512])
        pO = ps("pO", [P, 512])

        def T_bank(f):
            return (pL[:, 0, :], pL[:, 1, :], acc[0][:, 0, :], acc[0][:, 1, :])[f % 4]

        def sem(name):
            return ctx.enter_context(nc.semaphore(name))

        raw_landed = [sem(f"raw_landed{s}") for s in range(2)]
        hi_done = sem("hi_done")
        lo_done = sem("lo_done")
        unit_done = sem("unit_done")
        acc_free = sem("acc_free")
        x_ready = sem("x_ready")
        vec_landed = sem("vec_landed")
        bias_landed = sem("bias_landed")
        x_landed = sem("x_landed")
        pool_const = sem("pool_const")
        pool_chain = sem("pool_chain")
        dve_const = sem("dve_const")
        act_const = sem("act_const")
        vec_T = sem("vec_T")
        lbs = sem("lbs")
        lbs_act = sem("lbs_act")
        xT_full = sem("xT_full")
        xT_read = sem("xT_read")
        n_sq, n_sum, n_rs, n_xf, n_hi = (sem(n) for n in ("n_sq", "n_sum", "n_rs", "n_xf", "n_hi"))
        fz_act, fz_dve, q_act, q_dve, og_act, og_dve = (sem(n) for n in ("fz_act", "fz_dve", "q_act", "q_dve",
                                                                         "og_act", "og_dve"))
        prep_act, prep_dve, lev_D, lev_E, lev_X = (sem(n) for n in ("prep_act", "prep_dve", "lev_D", "lev_E", "lev_X"))
        L_full, L_free, M_full, M_free = (sem(n) for n in ("L_full", "L_free", "M_full", "M_free"))
        as_chain, vblk_ready, s_chain, sn_scaled = (sem(n) for n in ("as_chain", "vblk_ready", "s_chain", "sn_scaled"))
        o_full, o_sq, o_rs, o_norm, o_out = (sem(n) for n in ("o_full", "o_sq", "o_rs", "o_norm", "o_out"))
        s0_landed, state_stored = sem("s0_landed"), sem("state_stored")
        sqr_done, hid_hi = sem("sqr_done"), sem("hid_hi")
        ho_hi = sem("ho_hi")
        y_full, y_read = sem("y_full"), sem("y_read")
        y_stored = [sem(f"y_stored{n}") for n in range(2)]

        tri_done = sem("tri_done")
        pt_landed = sem("pt_landed")
        B_full, B_free, R_full, R_free, AV_full, AV_free = (sem(n) for n in ("B_full", "B_free", "R_full", "R_free",
                                                                             "AV_full", "AV_free"))
        k_hi, kq_lo, q_hi, soft, sp_done, u_hi, u_lo, la_done, a_done = (sem(n) for n in (
            "k_hi", "kq_lo", "q_hi", "soft", "sp_done", "u_hi", "u_lo", "la_done", "a_done"))
        new_chain = sem("new_chain")
        kts_done, kv_stored = sem("kts_done"), sem("kv_stored")
        new_full, new_dve, new_act, qblk_done = (sem(n) for n in ("new_full", "new_dve", "new_act", "qblk_done"))
        kp_landed = [sem(f"kp_landed{n}") for n in range(2)]
        vp_landed = [sem(f"vp_landed{n}") for n in range(2)]
        T_full, Ta_free, Td_free = sem("T_full"), sem("Ta_free"), sem("Td_free")
        zS_full, zS_dve, zS_act, RS_full, RS_dve, AVS_full, AVS_free = (sem(n) for n in (
            "zS_full", "zS_dve", "zS_act", "RS_full", "RS_dve", "AVS_full", "AVS_free"))
        ao_hi = sem("ao_hi")

        block = ctx.enter_context(nc.Block())

        U_IN, U_OUT, U_MLP0 = 0, 4 * NB, 5 * NB
        U_Q = U_MLP0 + 2 * FCH * NB
        U_KV = U_Q + NB
        U_OB = U_KV + 2 * NB
        U_MLP1 = U_OB + NB
        U_END = U_MLP1 + 2 * FCH * NB
        X_N0, X_HG, X_N1 = 0, NB, 2 * NB
        X_HID0 = 3 * NB
        X_Q = X_HID0 + FCH * NB
        X_KV = X_Q + NB
        X_OB = X_KV + NB
        X_N3 = X_OB + NB
        X_HID1 = X_N3 + NB
        n_norm = {"mix0": 0, "mlp0": 1, "mix1": 2, "mlp1": 3, "final": 4}
        n_app = {"mix0": 0, "mlp0": 1, "q": 2, "kv": 3, "mlp1": 4, "final": 5}

        w_in_v = w_in_a.rearrange("l (k p) (g n) -> p (l k) g n", p=P, g=4)
        w_out_v = w_out_a.rearrange("l (k p) n -> p (l k) n", p=P)
        w_kv_v = w_kv.rearrange("(k p) (g n) -> p k g n", p=P, g=2)
        w_q_v = w_q_b.rearrange("l (k p) n -> p (l k) n", p=P)
        w_ob_v = w_out_b.rearrange("l (k p) n -> p (l k) n", p=P)
        w_up_v = [w_up[n].rearrange("(k p) n -> p k n", p=P) for n in range(2)]
        w_down_v = [w_down[n].rearrange("(c k p) n -> p c k n", p=P, k=8) for n in range(2)]
        k_out = k_prompt.rearrange("a (c p) h d -> p (a c) (h d)", p=P)
        v_out = v_prompt.rearrange("a (c p) h d -> p (a c) (h d)", p=P)
        tok2 = "p (a b) -> p a b"

        @block.sync
        def _(sp):
            def panel(s, Pn, halves, first=False):
                if not first:
                    sp.wait_ge(lo_done, Pn - 1)
                for dst, src in halves:
                    sp.dma_start(dst, src).then_inc(raw_landed[s], 16)

            def plain(s, w, col):
                return [(wraw[s][:, 4 * q:4 * q + 4, :], w(q)[:, :, bass.ds(col, 256)]) for q in range(2)]

            def w_in_halves(s, h):
                parts = [(1, 0), (2, 3)][s]
                return [(wraw[s][:, :, n * P:(n + 1) * P], w_in_v[:, :, part, bass.ts(h, P)])
                        for n, part in enumerate(parts)]

            def square(Pb, w):
                with sp.Fori(0, 2) as i:
                    for s in range(2):
                        panel(s, Pb + 2 * i + s, plain(s, w, 512 * i + 256 * s))

            for s in range(2):
                panel(s, s, w_in_halves(s, 0), first=True)
            with sp.Fori(1, NB) as h:
                for s in range(2):
                    panel(s, 2 * h + s, w_in_halves(s, h))
            square(U_OUT // 2, lambda q: w_out_v[:, 4 * q:4 * q + 4, :])

            def mlp(n, Ub):
                with sp.Fori(0, FCH) as c:
                    with sp.Fori(0, 2) as i:
                        for s in range(2):
                            panel(s, Ub // 2 + 8 * c + 2 * i + s,
                                  plain(s, lambda q: w_up_v[n][:, 4 * q:4 * q + 4, :], 1024 * c + 512 * i + 256 * s))
                    with sp.Fori(0, 2) as i:
                        for s in range(2):
                            panel(s, Ub // 2 + 4 + 8 * c + 2 * i + s,
                                  plain(s, lambda q: w_down_v[n][:, bass.ds(c, 1), 4 * q:4 * q + 4, :].rearrange(
                                      "p c k n -> p (c k) n"), 512 * i + 256 * s))

            mlp(0, U_MLP0)
            square(U_Q // 2, lambda q: w_q_v[:, 4 * q:4 * q + 4, :])
            with sp.Fori(0, NPAIR // 2) as i:
                for s in range(2):
                    panel(s, U_KV // 2 + 2 * i + s,
                          [(wraw[s][:, :, n * P:(n + 1) * P], w_kv_v[:, :, n, bass.ds(256 * i + 128 * s, P)])
                           for n in range(2)])
            sp.dma_start(pt[:], page_table.rearrange("s g -> (s g)").rearrange("(a n) -> a n", a=1)).then_inc(pt_landed, 16)
            sp.wait_ge(pt_landed, 16)

            def pages(s, b, first):
                for g in range(NPG):
                    page = sp.value_load(pt[0:1, bass.ds(4 * s + g, 1)], min_val=0, max_val=cache_k.shape[0] - 1)
                    if g == 0 and not first:
                        sp.wait_ge(zS_full, s - 1)
                    sp.dma_start(Kp[b][:, g, :], cache_k[bass.ds(page, 1)].rearrange("a p h d -> p (a h d)")
                                 ).then_inc(kp_landed[b], 16)
                for g in range(NPG):
                    page = sp.value_load(pt[0:1, bass.ds(4 * s + g, 1)], min_val=0, max_val=cache_k.shape[0] - 1)
                    if g == 0 and not first:
                        sp.wait_ge(AVS_full, s - 1)
                    sp.dma_start(Vp[b][:, g, :], cache_v[bass.ds(page, 1)].rearrange("a p h d -> p (a h d)")
                                 ).then_inc(vp_landed[b], 16)

            for s in range(2):
                panel(s, U_OB // 2 + s, plain(s, lambda q: w_ob_v[:, 4 * q:4 * q + 4, :], 256 * s))
            sp.wait_ge(unit_done, U_OB)
            sp.wait_ge(AV_free, 2 * NPAIR + 1)
            sp.wait_ge(qblk_done, 4)
            for s in range(2):
                pages(s, s, True)
            with sp.Fori(1, NSEQ // 2) as i:
                for b in range(2):
                    pages(2 * i + b, b, False)
            for s in range(2):
                panel(s, U_OB // 2 + 2 + s, plain(s, lambda q: w_ob_v[:, 4 * q:4 * q + 4, :], 512 + 256 * s))
            mlp(1, U_MLP1)
            for n in range(SEQ // P + 1):
                sp.wait_ge(y_read, 2 * n + 2)
                if n < SEQ // P:
                    sp.dma_start(y_prompt[0, n * P:(n + 1) * P, :], yrow[n % 2][:]).then_inc(y_stored[n % 2], 16)
                else:
                    sp.dma_start(y_sample.rearrange("s n d -> (s n) d"), yrow[n % 2][0:SMP, :]).then_inc(y_stored[n % 2], 16)
            sp.wait_ge(y_stored[0], 48)
            sp.wait_ge(y_stored[1], 32)
            sp.wait_ge(kv_stored, 32 * NPAIR + 32)
            sp.wait_ge(state_stored, 32 * NB)

        @block.gpsimd
        def _(pool):
            chain = Count(pool_chain)

            def link(ins):
                pool.wait_ge(pool_chain, chain.inc(ins))

            link(pool.memset(ident[:], 0.0))
            link(pool.affine_select(out=ident[:], in_=ident[:], compare_op=ALU.not_equal, fill=1.0, base=0,
                                    pattern=[[-1, P]], channel_multiplier=1))
            pool.memset(ones[:], 1.0).then_inc(pool_const, 1)
            link(pool.memset(masks[:], 0.0))
            for n, m in enumerate(LEVELS):
                link(pool.memset(masks[:, n, :].rearrange("p (b j) -> p b j", j=2 * m)[:, :, m:2 * m], 1.0))
            for n, m in enumerate(LEVELS):
                nb = P // (2 * m)
                v = masks[:, n, :].rearrange("p (b j) -> p b j", j=2 * m)
                link(pool.affine_select(out=v, in_=v, compare_op=ALU.is_ge, fill=0.0, base=0,
                                        pattern=[[-2 * m, nb], [0, 2 * m]], channel_multiplier=1))
                link(pool.affine_select(out=v, in_=v, compare_op=ALU.is_ge, fill=0.0, base=m - 1,
                                        pattern=[[2 * m, nb], [0, 2 * m]], channel_multiplier=-1))
            link(pool.memset(scan_keep[:], 1.0))
            link(pool.memset(scan_keep[:, 0:SEQ:CH], 0.0))
            link(pool.memset(scan_keep[:, SEQ:T:NEW], 0.0))
            link(pool.memset(seqmask[:], 1.0))
            link(pool.affine_select(out=seqmask[:], in_=seqmask[:], compare_op=ALU.is_ge, fill=0.0, base=0,
                                    pattern=[[-NEW, NSEQ]], channel_multiplier=1))
            pool.affine_select(out=seqmask[:], in_=seqmask[:], compare_op=ALU.is_ge, fill=0.0, base=NEW - 1,
                               pattern=[[NEW, NSEQ]], channel_multiplier=-1).then_inc(pool_const, 1)
            link(pool.memset(tri_f[:], 1.0))
            link(pool.affine_select(out=tri_f[:], in_=tri_f[:], compare_op=ALU.is_ge, fill=0.0, base=0,
                                    pattern=[[-1, P]], channel_multiplier=1))
            link(pool.memset(neg_f[:], 0.0))
            link(pool.affine_select(out=neg_f[:], in_=neg_f[:], compare_op=ALU.is_ge, fill=NEG, base=-1,
                                    pattern=[[1, P]], channel_multiplier=-1))
            link(pool.memset(neg_s[:], 0.0))
            link(pool.affine_select(out=neg_s[:], in_=neg_s[:], compare_op=ALU.is_ge, fill=NEG, base=-1,
                                    pattern=[[1, SMP]], channel_multiplier=-1))
            v = neg_s[:].rearrange("p (s n) -> p s n", n=NEW)
            pool.affine_select(out=v, in_=v, compare_op=ALU.is_ge, fill=NEG, base=0,
                               pattern=[[-NEW, NSEQ], [0, NEW]], channel_multiplier=1).then_inc(pool_const, 1)
            with pool.Fori(0, U_END // 4) as i:
                for s in range(2):
                    pool.wait_ge(hi_done, 2 * i + s + 1)
                    pool.tensor_tensor(wlo[s][:], wraw[s][:], whi[s][:].bitcast(F32), ALU.subtract).then_inc(lo_done, 1)

        @block.scalar
        def _(act):
            act.preload_act_table_set("natural_log_exp_and_others")
            def wsplit(s, Pn, n_use, first=False):
                act.wait_ge(raw_landed[s], 32 * n_use)
                if not first:
                    act.wait_ge(unit_done, 2 * Pn - 2)
                act.activation(whi[s][:], wraw[s][:], ACT.Copy).then_inc(hi_done, 1)

            def wsplit_loop(Pb, n):
                with act.Fori(0, n) as i:
                    for s in range(2):
                        wsplit(s, Pb + 2 * i + s, Pb // 2 + 1 + i)

            act.dma_start(vec_rows[0:16, :], lb_logits.rearrange("a (m p) -> (a m) p", p=P)).then_inc(vec_landed, 16)
            for r, v in ((GON, g_onorm_a), (GMIX0, g_mix), (GMLP0, g_mlp)):
                n = v.shape[0] * NB
                act.dma_start(vec_rows[r:r + n, :], v.rearrange("a (m p) -> (a m) p", p=P)).then_inc(vec_landed, 16)
            for r, v in ((GKV, g_kv), (GFIN, g_final)):
                act.dma_start(vec_rows[r:r + NB, :], v.rearrange("(m p) -> m p", p=P)).then_inc(vec_landed, 16)
            act.dma_start(bias_row[:], sb_bias).then_inc(bias_landed, 16)
            act.dma_start(x_rows[:], x_prompt.rearrange("a (c p) d -> p (a c) d", p=P)).then_inc(x_landed, 16)
            act.dma_start(xs_rows[:], x_sample.rearrange("s n d -> (s n) d")).then_inc(x_landed, 16)
            act.dma_start(S0[:], state_hgrn[0, :, 0].rearrange("s k v -> k s v")).then_inc(s0_landed, 16)
            for s in range(2):
                wsplit(s, s, 1, first=True)
            act.wait_ge(pool_const, 1)
            act.activation(ones_r[:], ones[:], ACT.Copy).then_inc(act_const, 1)
            act.activation(ident_r[:], ident[:], ACT.Copy).then_inc(act_const, 1)
            act.wait_ge(lbs, 3)
            act.activation(small[:, 2 * NB:4 * NB], small[:, 0:2 * NB], ACT.Exp).then_inc(lbs_act, 1)
            for m in range(NB):
                act.wait_ge(xT_full, m + 1)
                act.activation(hT[:, m, 0:SEQ], pL[:, m % 2, :], ACT.Copy).then_inc(xT_read, 1)

            def norm_stats(call, ready):
                for m in range(NB):
                    ready(m)
                    act.activation(nrm[:, m, :], hT[:, m, :], ACT.Square).then_inc(n_sq, 1)
                act.wait_ge(n_sum, call + 1)
                act.activation(rstd[:].rearrange(tok2, a=2), pL[:, :, 0:HALF], ACT.Ln, scale=1.0 / DM,
                               bias=eps_t[:, 0:1]).then_inc(n_rs, 1)
                act.wait_ge(n_rs, 2 * call + 1)
                act.activation(rstd[:], rstd[:], ACT.Exp, scale=-0.5).then_inc(n_rs, 1)

            def norm_hi(app, dst):
                for m in range(NB):
                    act.wait_ge(n_xf, NB * app + m + 1)
                    act.activation(dst[:, m, :], nrm[:, m, :], ACT.Copy).then_inc(n_hi, 1)

            def x_block(m):
                act.wait_ge(xT_read, NB)
                act.wait_ge(dve_const, 4)

            norm_stats(0, x_block)
            norm_hi(0, xa_hi)
            act.wait_ge(pool_const, 3)
            act.activation(tri_r[:], tri_f[:], ACT.Copy).then_inc(tri_done, 1)
            act.activation(neg_r[:], neg_f[:], ACT.Copy).then_inc(tri_done, 1)

            def log_chain(src, dst, c, want):
                act.wait_ge(*want)
                act.wait_ge(c.sem, c.inc(act.activation(dst[:], src[:], ACT.Exp, scale=-1.0)))
                act.wait_ge(c.sem, c.inc(act.activation(dst[:], dst[:], ACT.Ln, bias=1.0)))

            def head_fz_q(h):
                c = Count(fz_act, 0, h, 5)
                cq = Count(q_act, 0, h, 3)
                log_chain(cl0, t1, c, (acc_free, 4 * h + 3))
                c.inc(act.activation(fg[:], t1[:], ACT.Exp, scale=-1.0))
                log_chain(qq, tq, cq, (acc_free, 4 * h + 4))
                cq.inc(act.activation(tq[:], tq[:], ACT.Exp, scale=-1.0))
                cq.end()
                act.wait_ge(fz_dve, 4 * h + 1)
                c.inc(act.activation(t2[:], t2[:], ACT.Exp, scale=-1.0))
                act.wait_ge(fz_dve, 4 * h + 2)
                c.inc(act.activation(fg[:], fg[:], ACT.Ln))
                c.end()

            def head_og(h):
                c = Count(og_act, 0, h, 3)
                log_chain(cl0, tq, c, (acc_free, 4 * h + 6))
                c.inc(act.activation(tq[:], tq[:], ACT.Exp, scale=-1.0))
                c.end()

            def head_prep(h):
                act.wait_ge(fz_dve, 4 * h + 4)
                act.activation(eG[:], G[:], ACT.Exp).then_inc(prep_act, 1)
                act.wait_ge(prep_dve, 4 * h + 1)
                act.activation(ek[:], ek[:], ACT.Exp).then_inc(prep_act, 1)
                for n in range(len(LEVELS)):
                    act.wait_ge(lev_D, len(LEVELS) * h + n + 1)
                    act.activation(D[n % 2][:, 0:TW[n]], D[n % 2][:, 0:TW[n]], ACT.Exp).then_inc(lev_E, 1)

            def head_finish(h):
                act.wait_ge(o_full, h + 1)
                act.activation(t1[:, 0:SEQ], pO[:], ACT.Square).then_inc(o_sq, 1)
                act.wait_ge(M_full, 4 * h + 3)
                act.activation(t1[:, SEQ:T], pM[:, 0:SMP], ACT.Square).then_inc(o_sq, 1)
                act.wait_ge(L_full, 14 * h + 14)
                act.wait_ge(L_free, 14 * h + 13)
                act.activation(rstd[:, 0:SEQ], pL[:, 1, :], ACT.Ln, scale=1.0 / P, bias=eps_t[:, 0:1]).then_inc(L_free, 1)
                act.wait_ge(M_full, 4 * h + 4)
                act.activation(rstd[:, SEQ:T], pM[:, SMP:2 * SMP], ACT.Ln, scale=1.0 / P,
                               bias=eps_t[:, 0:1]).then_inc(o_rs, 1)
                act.wait_ge(L_free, 14 * h + 14)
                act.wait_ge(o_rs, 2 * h + 1)
                act.activation(rstd[:], rstd[:], ACT.Exp, scale=-0.5).then_inc(o_rs, 1)

            def states_out(h):
                act.wait_ge(o_out, h + 1)
                act.dma_start(st_prompt[0, 0, bass.ds(h, 1)].rearrange("a k v -> k (a v)"), S[:, NCH - 1, :]
                              ).then_inc(state_stored, 16)
                act.dma_start(st_sample[0][:, bass.ds(h, 1)].rearrange("s a k v -> k (s a) v"), Sn[:]
                              ).then_inc(state_stored, 16)

            def head_units(h, lag):
                head_fz_q(h)
                wsplit(0, 2 * h + 2, h + 2)
                if lag is not None:
                    head_finish(lag)
                    act.wait_ge(o_out, h)
                head_prep(h)
                if lag is not None:
                    states_out(lag)
                    act.dma_start(S0[:], state_hgrn[0][:, bass.ds(h, 1)].rearrange("s a k v -> k (s a) v")
                                  ).then_inc(s0_landed, 16)
                head_og(h)
                wsplit(1, 2 * h + 3, h + 2)

            head_units(0, None)
            with act.Fori(1, NB) as h:
                head_units(h, h - 1)
            head_finish(NB - 1)
            states_out(NB - 1)
            for m in range(NB):
                act.activation(xa_hi[:, m, :], hgrn_o[:, m, :], ACT.Copy).then_inc(ho_hi, 1)
            wsplit_loop(U_OUT // 2 + 2, 2)

            def h_block(U):
                return lambda m: act.wait_ge(acc_free, U + m + 3)

            def mlp(Ub, Hb, norm_call, app, last):
                norm_stats(norm_call, h_block(Ub - NB))
                norm_hi(app, xa_hi)

                def chunk(c, n_split):
                    with act.Fori(0, 2) as i:
                        for s in range(2):
                            for a in range(2):
                                U = Ub + 16 * c + 4 * i + 2 * s + a
                                n = Hb + NB * c + 4 * i + 2 * s + a
                                act.wait_ge(unit_done, U + 1)
                                act.wait_ge(acc_free, U + 2)
                                act.activation(relu_t[a][:].rearrange(tok2, a=2), acc[a][:, :, 0:HALF], ACT.Relu
                                               ).then_inc(acc_free, 1)
                                act.wait_ge(sqr_done, n + 1)
                                act.activation(xb_hi[:, bass.ds(4 * i + 2 * s + a, 1), :].rearrange("p a t -> p (a t)"),
                                               sqr_t[a][:], ACT.Copy).then_inc(hid_hi, 1)
                            wsplit(s, Ub // 2 + 8 * c + 2 * i + s + 2, Ub // 4 + 4 * c + i + 2)
                    with act.Fori(0, n_split) as i:
                        for s in range(2):
                            wsplit(s, Ub // 2 + 8 * c + 4 + 2 * i + s + 2, Ub // 4 + 4 * c + i + 4)

                with act.Fori(0, FCH - last) as c:
                    chunk(c, 2)
                if last:
                    chunk(FCH - 1, 1)

            mlp(U_MLP0, 0, n_norm["mlp0"], n_app["mlp0"], 0)
            norm_stats(n_norm["mix1"], h_block(U_Q - NB))
            norm_hi(n_app["q"], xa_hi)
            norm_hi(n_app["kv"], xb_hi)
            wsplit_loop(U_Q // 2 + 2, 2)

            def soft3(src, dst, n, sm):
                act.activation(dst, src, ACT.Abs).then_inc(sm, 1)
                act.wait_ge(sm, n + 1)
                act.activation(dst, dst, ACT.Exp, scale=-1.0).then_inc(sm, 1)
                act.wait_ge(sm, n + 2)
                act.activation(dst, dst, ACT.Ln, bias=1.0).then_inc(sm, 1)

            def pair(j, par, nxt):
                act.wait_ge(acc_free, U_KV + 2 * j + 3)
                act.activation(khi[:], kf[:], ACT.Copy).then_inc(k_hi, 1)
                act.activation(qhi[:], qT[:, bass.ds(j, 1), 0:SEQ].rearrange("p a t -> p (a t)"), ACT.Copy).then_inc(q_hi, 1)
                act.wait_ge(B_free, 8 * j + 2 + 2)
                act.dma_start(k_out[:, :, bass.ds(j * P, P)], kr[:]).then_inc(kv_stored, 16)
                act.dma_start(v_out[:, :, bass.ds(j * P, P)], vr[:]).then_inc(kv_stored, 16)
                for n in range(7):
                    N = 6 * j + n
                    if n >= 1:
                        hh, g = divmod(n - 1, 3)
                        cols = slice(GCOL[g], GCOL[g] + GW[g])
                        act.wait_ge(sp_done, N)
                        act.activation(uh[hh][:, cols], tl[(n - 1) % 2][:, 0:GW[g]], ACT.Copy).then_inc(u_hi, 1)
                    if n < 6:
                        g = n % 3
                        act.wait_ge(B_free, 8 * j + n + 5)
                        soft3(zb[n % 2][:, 0:GW[g]], tl[n % 2][:, 0:GW[g]], 3 * N, soft)
                    if n >= 1:
                        hh, g = divmod(n - 1, 3)
                        if (hh, g) == (1, 0):
                            act.wait_ge(AV_full, 2 * j + 1)
                        act.wait_ge(la_done, N + 1)
                        act.activation(Am[:, GCOL[g]:GCOL[g] + GW[g]], zb[(n - 1) % 2][:, 0:GW[g]], ACT.Exp
                                       ).then_inc(a_done, 1)

            def pair_split(par, i, j):
                wsplit(1 - par, U_KV // 2 + j + 3, U_KV // 4 + i + 2 + par)

            wsplit(0, U_KV // 2 + 2, U_KV // 4 + 2)
            with act.Fori(0, NPAIR // 2 - 1) as i:
                for par in range(2):
                    pair(2 * i + par, par, True)
                    pair_split(par, i, 2 * i + par)
            pair(NPAIR - 2, 0, True)
            pair_split(0, NPAIR // 2 - 1, NPAIR - 2)
            pair(NPAIR - 1, 1, False)

            act.wait_ge(new_dve, 2)
            soft3(zbN[:], tlN[:], 0, new_act)
            act.wait_ge(new_dve, 3)
            act.activation(uhN[:], tlN[:], ACT.Copy).then_inc(new_act, 1)
            act.dma_start(k_sample.rearrange("s n h d -> (s n) (h d)"), kvn[:, 0].rearrange("p j f -> p (j f)")
                          ).then_inc(kv_stored, 16)
            act.dma_start(v_sample.rearrange("s n h d -> (s n) (h d)"), kvn[:, 1].rearrange("p j f -> p (j f)")
                          ).then_inc(kv_stored, 16)
            act.wait_ge(new_dve, 5)
            act.wait_ge(kv_stored, 32 * NPAIR + 32)
            act.activation(AN[:], zbN[:], ACT.Exp).then_inc(new_act, 1)

            def t_copy(s, f):
                act.wait_ge(T_full, 8 * s + f + 1)
                act.activation(KT[:, 4 * (f % 2):4 * (f % 2) + 4, f // 2, :],
                               T_bank(f).rearrange("p (j k) -> p j k", k=P), ACT.Copy).then_inc(Ta_free, 1)

            def seq(s, nxt):
                act.wait_ge(zS_dve, 4 * s + 1)
                soft3(zbS[:], tlS[:], 5 * s, zS_act)
                if nxt:
                    t_copy(s + 1, 0)
                    t_copy(s + 1, 2)
                act.wait_ge(zS_dve, 4 * s + 2)
                act.activation(uhS[:], tlS[:], ACT.Copy).then_inc(zS_act, 1)
                if nxt:
                    t_copy(s + 1, 4)
                act.wait_ge(zS_dve, 4 * s + 4)
                act.activation(AS[:], zbS[:], ACT.Exp).then_inc(zS_act, 1)
                if nxt:
                    t_copy(s + 1, 6)

            for f in (0, 2, 4, 6):
                t_copy(0, f)
            with act.Fori(0, NSEQ - 1) as s:
                seq(s, True)
            seq(NSEQ - 1, False)
            for m in range(NB):
                act.wait_ge(AVS_free, 2 * NSEQ + 2)
                act.activation(xb_hi[:, m, :], attn_o[:, m, :], ACT.Copy).then_inc(ao_hi, 1)
            wsplit_loop(U_OB // 2 + 2, 2)
            mlp(U_MLP1, FCH * NB, n_norm["mlp1"], n_app["mlp1"], 1)
            norm_stats(n_norm["final"], h_block(U_END - NB))
            for n in range(SEQ // P + 1):
                w = P if n < SEQ // P else SMP
                act.wait_ge(y_full, 2 * n + 1)
                if n:
                    act.wait_ge(y_read, 2 * n)
                if n >= 2:
                    act.wait_ge(y_stored[n % 2], 16 * (n // 2))
                act.activation(yrow[n % 2][0:w, 0:512], pL[0:w, 0, :], ACT.Copy).then_inc(y_read, 1)

        @block.vector
        def _(dve):
            def lo_part(dst, hi, full, sem_hi, count):
                dve.wait_ge(sem_hi, count)
                dve.tensor_tensor(dst, full, hi.bitcast(F32), ALU.subtract).then_inc(x_ready, 1)

            for n, q in enumerate((B_free, B_free, a_done, a_done, AV_free, la_done, AVS_free, AVS_free)):
                dve.memset(start_mark[0:1, n:n + 1], 0.0).then_inc(q, 1)
            dve.memset(eps_t[:], EPS).then_inc(acc_free, 1)
            dve.memset(Amat[:], 0.0).then_inc(acc_free, 1)
            dve.memset(As[:], 0.0).then_inc(dve_const, 1)
            dve.wait_ge(vec_T, 1)
            dve.tensor_copy(gT[:], pO[:, 0:72]).then_inc(dve_const, 1)
            dve.tensor_copy(bias_h[:], pO[:, 72:72 + H_B]).then_inc(dve_const, 1)
            dve.wait_ge(dve_const, 2)
            dve.tensor_tensor(small[:, 2 * NB:3 * NB], gT[:, LB0:LB0 + NB], gT[:, LB1:LB1 + NB], ALU.max).then_inc(lbs, 1)
            dve.wait_ge(lbs, 1)
            dve.tensor_tensor(small[:, 0:NB], gT[:, LB0:LB0 + NB], small[:, 2 * NB:3 * NB], ALU.subtract).then_inc(lbs, 1)
            dve.tensor_tensor(small[:, NB:2 * NB], gT[:, LB1:LB1 + NB], small[:, 2 * NB:3 * NB], ALU.subtract).then_inc(lbs, 1)
            dve.wait_ge(lbs_act, 1)
            dve.tensor_tensor(small[:, 0:NB], small[:, 2 * NB:3 * NB], small[:, 3 * NB:4 * NB], ALU.add).then_inc(lbs, 1)
            dve.wait_ge(lbs, 4)
            dve.reciprocal(small[:, NB:2 * NB], small[:, 0:NB]).then_inc(lbs, 1)
            dve.wait_ge(lbs, 5)
            dve.tensor_tensor(small[:, 2 * NB:3 * NB], small[:, 2 * NB:3 * NB], small[:, NB:2 * NB], ALU.mult).then_inc(lbs, 1)
            dve.tensor_tensor(omlb[:], small[:, 3 * NB:4 * NB], small[:, NB:2 * NB], ALU.mult).then_inc(lbs, 1)
            dve.wait_ge(lbs, 6)
            dve.tensor_scalar(lb[:], small[:, 2 * NB:3 * NB], 2.0 ** -60, None, ALU.max).then_inc(lbs, 1)
            dve.wait_ge(xT_full, NB + 1)
            dve.tensor_copy(hT[:, :, SEQ:T], pM[:].rearrange("p (m t) -> p m t", t=SMP)).then_inc(dve_const, 1)

            def norm_apply(call, app, g, hi, lo):
                dve.wait_ge(n_rs, 2 * call + 2)
                for m in range(NB):
                    dve.scalar_tensor_tensor(out=nrm[:, m, :], in0=hT[:, m, :], scalar=gT[:, g + m:g + m + 1],
                                             in1=rstd[:], op0=ALU.mult, op1=ALU.mult).then_inc(n_xf, 1)
                for m in range(NB):
                    dve.wait_ge(n_xf, NB * app + m + 1)
                    lo_part(lo[:, m, :], hi[:, m, :], nrm[:, m, :], n_hi, NB * app + m + 1)

            norm_apply(n_norm["mix0"], n_app["mix0"], GMIX0, xa_hi, xa_lo)

            def accv(a):
                return acc[a][:, :, 0:HALF]

            def t2v(t):
                return t[:].rearrange(tok2, a=2)

            def head_gates(h):
                if not isinstance(h, int) or h:
                    dve.wait_ge(og_dve, h)
                dve.wait_ge(unit_done, 4 * h + 1)
                dve.tensor_scalar(t2v(cl0), accv(0), CLAMP, None, ALU.max).then_inc(acc_free, 1)
                dve.wait_ge(unit_done, 4 * h + 2)
                dve.tensor_scalar(t2v(qq), accv(1), CLAMP, None, ALU.max).then_inc(acc_free, 1)

            def head_fz_q(h, step):
                if step == 0:
                    dve.wait_ge(fz_act, 5 * h + 2)
                    dve.wait_ge(acc_free, 4 * h + 3)
                    dve.tensor_tensor(t2[:], cl0[:], t1[:], ALU.add).then_inc(fz_dve, 1)
                if step == 1:
                    dve.wait_ge(fz_act, 5 * h + 3)
                    dve.tensor_scalar(fg[:], fg[:], omlb[:, bass.ds(h, 1)], lb[:, bass.ds(h, 1)], ALU.mult, ALU.add
                                      ).then_inc(fz_dve, 1)
                if step == 2:
                    dve.wait_ge(q_act, 3 * h + 3)
                    dve.wait_ge(acc_free, 4 * h + 4)
                    dve.tensor_tensor(qq[:], qq[:], tq[:], ALU.mult).then_inc(q_dve, 1)
                if step == 3:
                    dve.wait_ge(fz_act, 5 * h + 4)
                    dve.tensor_scalar(kk[:], t2[:], omlb[:, bass.ds(h, 1)], None, ALU.mult).then_inc(fz_dve, 1)
                if step == 4:
                    dve.wait_ge(fz_act, 5 * h + 5)
                    dve.tensor_tensor_scan(G[:], scan_keep[:], fg[:], 0.0, ALU.mult, ALU.add).then_inc(fz_dve, 1)

            def head_v(h):
                dve.wait_ge(unit_done, 4 * h + 3)
                dve.tensor_copy(t2v(vT), accv(0)).then_inc(acc_free, 1)

            def head_og(h):
                dve.wait_ge(unit_done, 4 * h + 4)
                dve.tensor_scalar(t2v(cl0), accv(1), CLAMP, None, ALU.max).then_inc(acc_free, 1)
                dve.wait_ge(og_act, 3 * h + 3)
                dve.wait_ge(acc_free, 4 * h + 6)
                dve.scalar_tensor_tensor(out=sgg[:], in0=cl0[:], scalar=gT[:, bass.ds(GON + h, 1)], in1=tq[:],
                                         op0=ALU.mult, op1=ALU.mult).then_inc(og_dve, 1)

            def head_prep(h):
                c = Count(prep_dve, 0, h, 4)
                dve.wait_ge(fz_dve, 4 * h + 4)
                dve.wait_ge(q_dve, h + 1)
                Gp = G[:, 0:SEQ].rearrange("p (c t) -> p c t", t=CH)
                Gs = G[:, SEQ:T].rearrange("p (c t) -> p c t", t=NEW)
                ekp = ek[:, 0:SEQ].rearrange("p (c t) -> p c t", t=CH)
                eks = ek[:, SEQ:T].rearrange("p (c t) -> p c t", t=NEW)
                dve.tensor_tensor(ekp, Gp[:, :, CH - 1:CH].to_broadcast([P, NCH, CH]), Gp, ALU.subtract)
                c.inc(dve.tensor_tensor(eks, Gs[:, :, NEW - 1:NEW].to_broadcast([P, NSEQ, NEW]), Gs, ALU.subtract))
                n_lv = len(LEVELS)

                def diffs(n):
                    m, w = LEVELS[n], TW[n]
                    if n >= 2:
                        dve.wait_ge(lev_X, 2 * n_lv * h + 2 * (n - 2) + 2)
                    Gv = G[:, 0:w].rearrange("p (b j) -> p b j", j=2 * m)
                    Dv = D[n % 2][:, 0:w].rearrange("p (b j) -> p b j", j=2 * m)
                    mid = Gv[:, :, m - 1:m].to_broadcast([P, w // (2 * m), m])
                    dve.tensor_tensor(Dv[:, :, 0:m], mid, Gv[:, :, 0:m], ALU.subtract)
                    dve.tensor_tensor(Dv[:, :, m:2 * m], Gv[:, :, m:2 * m], mid, ALU.subtract).then_inc(lev_D, 1)

                def factors(n):
                    m, w = LEVELS[n], TW[n]
                    dve.wait_ge(lev_E, n_lv * h + n + 1)
                    Ev = D[n % 2][:, 0:w].rearrange("p (b j) -> p b j", j=2 * m)
                    Xv = X[n][:, 0:w].rearrange("p (b j) -> p b j", j=2 * m)
                    kv = kk[:, 0:w].rearrange("p (b j) -> p b j", j=2 * m)
                    qv = qq[:, 0:w].rearrange("p (b j) -> p b j", j=2 * m)
                    dve.tensor_tensor(Xv[:, :, 0:m], Ev[:, :, 0:m], kv[:, :, 0:m], ALU.mult).then_inc(lev_X, 1)
                    dve.tensor_tensor(Xv[:, :, m:2 * m], Ev[:, :, m:2 * m], qv[:, :, m:2 * m], ALU.mult).then_inc(lev_X, 1)

                diffs(0)
                c.inc(dve.tensor_tensor(dg[:], qq[:], kk[:], ALU.mult))
                dve.wait_ge(prep_act, 2 * h + 1)
                c.inc(dve.tensor_tensor(qe[:], qq[:], eG[:], ALU.mult))
                dve.wait_ge(prep_act, 2 * h + 2)
                c.inc(dve.tensor_tensor(kh[:], kk[:], ek[:], ALU.mult))
                c.end()
                for n in range(n_lv):
                    if n + 1 < n_lv:
                        diffs(n + 1)
                    factors(n)
                    if n == 2:
                        head_v(h)

            def head_products(h, first, nxt):
                if nxt is not None:
                    head_gates(nxt)
                Lb, Mb = 14 * h, 4 * h
                for n in range(2):
                    dve.wait_ge(L_full, Lb + n + 1)
                    dve.tensor_copy(VK[:, n, 0:NCH, :], pL[:, n, :].rearrange("p (c d) -> p c d", d=P)).then_inc(L_free, 1)
                dve.wait_ge(M_full, Mb + 1)
                dve.tensor_copy(VK[0:SMP, :, NCH, :], pM[0:SMP, 0:2 * P].rearrange("p (n d) -> p n d", d=P)
                                ).then_inc(M_free, 1)
                for n in range(len(LEVELS) + 1):
                    mk = (masks[:, n:n + 1, :] if n < len(LEVELS) else ident[:].rearrange("p (a t) -> p a t", a=1))
                    dve.wait_ge(L_free, Lb + n + 2)
                    dve.wait_ge(L_full, Lb + n + 3)
                    dve.memset(wait_mark[0:1, n:n + 1], 0.0)
                    dve.copy_predicated(Amat[:], mk.to_broadcast([P, NCH, P]).bitcast(U32),
                                        pL[:, n % 2, :].rearrange("p (c t) -> p c t", t=P)).then_inc(L_free, 1)
                    if nxt is not None and n < 5:
                        head_fz_q(nxt, n)
                dve.wait_ge(M_full, Mb + 2)
                dve.memset(wait_mark[0:1, 15:16], 0.0)
                for n in range(SMP_LEVELS + 1):
                    mk = masks[0:SMP, len(LEVELS) - SMP_LEVELS + n, 0:SMP] if n < SMP_LEVELS else ident[0:SMP, 0:SMP]
                    if n:
                        dve.wait_ge(as_chain, SMP_LEVELS * h + n)
                        dve.memset(wait_mark[0:1, 10 + n:11 + n], 0.0)
                    dve.copy_predicated(As[:], mk.bitcast(U32), pM[0:SMP, 2 * P + n * SMP:2 * P + (n + 1) * SMP]
                                        ).then_inc(as_chain if n < SMP_LEVELS else M_free, 1)
                dve.wait_ge(M_free, 3 * h + 1)
                dve.tensor_tensor(Vblk[:], VK[0:SMP, 0, NCH:NCH + 1, :].to_broadcast([SMP, NSEQ, P]),
                                  seqmask[:].rearrange("p (s a) -> p s a", a=1).to_broadcast([SMP, NSEQ, P]), ALU.mult
                                  ).then_inc(vblk_ready, 1)
                dve.wait_ge(L_full, Lb + 11)
                if not first:
                    dve.wait_ge(state_stored, 32 * h)
                for n in range(NCH):
                    kv = pL[:, 0, n * P:(n + 1) * P]
                    if n == 0:
                        dve.tensor_copy(S[:, 0, :], kv).then_inc(s_chain, 1)
                        continue
                    dve.wait_ge(s_chain, 3 * h + n)
                    ins = dve.scalar_tensor_tensor(out=S[:, n, :], in0=S[:, n - 1, :],
                                                   scalar=eG[:, n * CH + CH - 1:n * CH + CH], in1=kv,
                                                   op0=ALU.mult, op1=ALU.add)
                    ins.then_inc(s_chain if n < NCH - 1 else L_free, 1)
                dve.wait_ge(s0_landed, 16 * h + 16)
                dve.tensor_tensor(Sn[:], S0[:], eG[:, SEQ + NEW - 1:T:NEW].rearrange("p (s a) -> p s a", a=1)
                                  .to_broadcast([P, NSEQ, P]), ALU.mult).then_inc(sn_scaled, 1)
                dve.wait_ge(sn_scaled, h + 1)
                for n in range(2):
                    dve.wait_ge(L_full, Lb + 12 + n)
                    dve.tensor_tensor(Sn[:, 4 * n:4 * n + 4, :], Sn[:, 4 * n:4 * n + 4, :],
                                      pL[:, (n + 1) % 2, :].rearrange("p (s v) -> p s v", v=P), ALU.add).then_inc(L_free, 1)
                dve.wait_ge(o_rs, 2 * h + 2)
                dve.tensor_tensor(t2[:, 0:SEQ], pO[:], rstd[:, 0:SEQ], ALU.mult).then_inc(o_norm, 1)
                dve.tensor_tensor(t2[:, SEQ:T], pM[:, 0:SMP], rstd[:, SEQ:T], ALU.mult).then_inc(M_free, 1)
                dve.wait_ge(o_norm, h + 1)
                dve.wait_ge(M_free, 3 * h + 3)
                dve.wait_ge(og_dve, h + 1)
                dve.tensor_tensor(hgrn_o[:, bass.ds(h, 1), :].rearrange("p a t -> p (a t)"), t2[:], sgg[:], ALU.mult
                                  ).then_inc(o_out, 1)

            dve.wait_ge(pool_const, 2)
            head_gates(0)
            for n in range(5):
                head_fz_q(0, n)
            head_prep(0)
            head_og(0)
            head_products(0, True, 1)
            head_prep(1)
            head_og(1)
            with dve.Fori(2, NB) as h:
                head_products(h - 1, False, h)
                head_prep(h)
                head_og(h)
            head_products(NB - 1, False, None)
            for m in range(NB):
                lo_part(xa_lo[:, m, :], xa_hi[:, m, :], hgrn_o[:, m, :], ho_hi, m + 1)

            def add_to_h(Ub):
                with dve.Fori(0, 4) as i:
                    for a in range(2):
                        hv = hT[:, bass.ds(2 * i + a, 1), :].rearrange("p o (a b) -> p (o a) b", a=2)
                        dve.wait_ge(unit_done, Ub + 2 * i + a + 1)
                        dve.tensor_tensor(hv, hv, accv(a), ALU.add).then_inc(acc_free, 1)

            add_to_h(U_OUT)

            def mlp(Ub, Hb, hid_hi_t, hid_lo_t):
                with dve.Fori(0, FCH) as c:
                    with dve.Fori(0, 4) as i:
                        for a in range(2):
                            n = Hb + NB * c + 2 * i + a
                            hb = bass.ds(2 * i + a, 1)
                            dve.wait_ge(acc_free, Ub + 16 * c + 2 * i + a + 3)
                            dve.tensor_tensor(sqr_t[a][:], relu_t[a][:], relu_t[a][:], ALU.mult).then_inc(sqr_done, 1)
                            dve.wait_ge(sqr_done, n + 1)
                            lo_part(hid_lo_t[:, hb, :].rearrange("p a t -> p (a t)"),
                                    hid_hi_t[:, hb, :].rearrange("p a t -> p (a t)"), sqr_t[a][:], hid_hi, n + 1)
                    add_to_h(Ub + 16 * c + 8)

            norm_apply(n_norm["mlp0"], n_app["mlp0"], GMLP0, xa_hi, xa_lo)
            dve.wait_ge(state_stored, 32 * NB)
            mlp(U_MLP0, 0, xb_hi, xb_lo)
            norm_apply(n_norm["mix1"], n_app["q"], GMIX1, xa_hi, xa_lo)
            dve.wait_ge(n_hi, NB * n_app["kv"])
            dve.wait_ge(x_ready, X_KV)
            norm_apply(n_norm["mix1"], n_app["kv"], GKV, xb_hi, xb_lo)
            with dve.Fori(0, 4) as i:
                for a in range(2):
                    dve.wait_ge(unit_done, U_Q + 2 * i + a + 1)
                    dve.tensor_copy(qT[:, bass.ds(2 * i + a, 1), :].rearrange("p o (a b) -> p (o a) b", a=2), accv(a)
                                    ).then_inc(acc_free, 1)

            def kv_copy(U, a):
                dve.wait_ge(unit_done, U + a + 1)
                dve.tensor_copy(t2v((kf, vf)[a]), accv(a)).then_inc(acc_free, 1)

            def pair(j, nxt):
                U = U_KV + 2 * j
                dve.wait_ge(acc_free, U + 3)
                dve.tensor_copy(kTs[:, bass.ds(j, 1), :].rearrange("p a t -> p (a t)"), kf[:, SEQ:T]).then_inc(kts_done, 1)
                dve.wait_ge(k_hi, j + 1)
                dve.tensor_tensor(klo[:], kf[:], khi[:].bitcast(F32), ALU.subtract).then_inc(kq_lo, 1)
                dve.wait_ge(q_hi, j + 1)
                dve.tensor_tensor(qlo[:], qT[:, bass.ds(j, 1), 0:SEQ].rearrange("p a t -> p (a t)"),
                                  qhi[:].bitcast(F32), ALU.subtract).then_inc(kq_lo, 1)
                if not isinstance(j, int) or j:
                    dve.wait_ge(kv_stored, 32 * j)
                for n, t in enumerate((kr, vr)):
                    dve.wait_ge(B_full, 8 * j + n + 1)
                    dve.tensor_copy(t[:], pL[:, n, :].rearrange("p (c f) -> p c f", f=P)).then_inc(B_free, 1)
                dve.wait_ge(R_full, 7 * j + 1)
                dve.tensor_copy(kvn[:, :, bass.ds(j, 1), :].rearrange("p n a f -> p n (a f)"),
                                pM[0:SMP, 0:2 * P].rearrange("p (n f) -> p n f", f=P)).then_inc(R_free, 1)
                for n in range(7):
                    N = 6 * j + n
                    if n < 6:
                        hh, g = divmod(n, 3)
                        dve.wait_ge(a_done, N + 1)
                        dve.wait_ge(B_full, 8 * j + n + 3)
                        dve.tensor_scalar(zb[n % 2][:, 0:GW[g]], pL[:, n % 2, 0:GW[g]], SCALE,
                                          bias_h[:, bass.ds(2 * j + hh, 1)], ALU.mult, ALU.add).then_inc(B_free, 1)
                    if n >= 1:
                        hh, g = divmod(n - 1, 3)
                        cols = slice(GCOL[g], GCOL[g] + GW[g])
                        dve.wait_ge(u_hi, N)
                        dve.tensor_tensor(ul[hh][:, cols], tl[(n - 1) % 2][:, 0:GW[g]],
                                          uh[hh][:, cols].bitcast(F32), ALU.subtract).then_inc(u_lo, 1)
                        zv = zb[(n - 1) % 2][:, 0:GW[g]]
                        dve.wait_ge(sp_done, N)
                        dve.wait_ge(R_full, 7 * j + n + 1)
                        dve.tensor_tensor(zv, zv, pM[:, 0:GW[g]], ALU.subtract).then_inc(la_done, 1)
                    if n < 6:
                        g = n % 3
                        dve.wait_ge(soft, 3 * N + 3)
                        dve.wait_ge(B_free, 8 * j + n + 5)
                        tv = tl[n % 2][:, 0:GW[g]]
                        dve.scalar_tensor_tensor(out=tv, in0=zb[n % 2][:, 0:GW[g]], scalar=0.0, in1=tv,
                                                 op0=ALU.max, op1=ALU.add).then_inc(sp_done, 1)
                    if nxt and n in (2, 5):
                        kv_copy(U + 2, (n - 2) // 3)
                    if n in (4, 6):
                        hh = n // 2 - 2
                        rows = slice(64 * hh, 64 * hh + 64)
                        dve.wait_ge(AV_full, 2 * j + hh + 1)
                        dve.tensor_copy(attn_o[rows, bass.ds(j, 1), 0:SEQ].rearrange("p a t -> p (a t)"), pO[rows, :]
                                        ).then_inc(AV_free, 1)

            kv_copy(U_KV, 0)
            kv_copy(U_KV, 1)
            pair(0, True)
            with dve.Fori(1, NPAIR - 1) as j:
                pair(j, True)
            pair(NPAIR - 1, False)

            dve.wait_ge(AV_free, 2 * NPAIR + 1)
            dve.wait_ge(kv_stored, 32 * NPAIR)
            dve.memset(qblk[:], 0.0).then_inc(qblk_done, 1)
            dve.wait_ge(qblk_done, 1)
            for hh in range(2):
                rows = slice(64 * hh, 64 * hh + 64)
                dve.tensor_copy(qblk[rows, :, :, hh * NEW:(hh + 1) * NEW],
                                qT[rows, :, SEQ:T].rearrange("p j (s n) -> p j s n", n=NEW)).then_inc(qblk_done, 1)
            bcol = bias_h[:].rearrange("p (h a) -> p h a", a=1)
            dve.tensor_copy(biasQ[:].rearrange("p (h n) -> p h n", n=NEW), bcol.to_broadcast([P, H_B, NEW])
                            ).then_inc(new_chain, 1)
            dve.tensor_tensor(biasN[:], bcol[0:SMP].to_broadcast([SMP, H_B, SMP]),
                              neg_s[:].rearrange("p (a t) -> p a t", a=1).to_broadcast([SMP, H_B, SMP]), ALU.add
                              ).then_inc(new_chain, 1)
            dve.wait_ge(new_chain, 2)
            dve.wait_ge(new_full, 1)
            zN = pL[0:SMP].rearrange("p a b -> p (a b)")
            zbNf, tlNf = (t[:].rearrange("p h t -> p (h t)") for t in (zbN, tlN))
            for e in range(2):
                zb_e, bias_e = (t[:].rearrange("p (j e) t -> p j e t", e=2)[:, :, e, :] for t in (zbN, biasN))
                dve.scalar_tensor_tensor(out=zb_e, in0=pL[0:SMP, e, :].rearrange("p (j t) -> p j t", t=SMP),
                                         scalar=SCALE, in1=bias_e, op0=ALU.mult, op1=ALU.add).then_inc(new_dve, 1)
            dve.wait_ge(new_dve, 2)
            dve.wait_ge(new_act, 3)
            dve.scalar_tensor_tensor(out=tlNf, in0=zbNf, scalar=0.0, in1=tlNf, op0=ALU.max, op1=ALU.add).then_inc(new_dve, 1)
            dve.wait_ge(new_dve, 3)
            dve.wait_ge(new_act, 4)
            dve.tensor_tensor(ulN[:], tlN[:], uhN[:].bitcast(F32), ALU.subtract).then_inc(new_dve, 1)
            dve.wait_ge(new_full, 2)
            dve.tensor_tensor(zbNf, zbNf, zN, ALU.subtract).then_inc(new_dve, 1)
            dve.wait_ge(new_dve, 5)
            dve.wait_ge(new_act, 5)
            dve.memset(wait_mark[0:1, 0:1], 0.0).then_inc(qblk_done, 1)

            def t_copy(s, f):
                dve.wait_ge(T_full, 8 * s + f + 1)
                dve.tensor_copy(KT[:, 4 * (f % 2):4 * (f % 2) + 4, f // 2, :],
                                T_bank(f).rearrange("p (j k) -> p j k", k=P)).then_inc(Td_free, 1)

            def seq(s, nxt):
                dve.wait_ge(zS_full, s + 1)
                dve.scalar_tensor_tensor(out=zbS[:].rearrange("p (g c) -> p g c", c=P),
                                         in0=pM[:].rearrange("p (g c) -> p g c", c=P), scalar=SCALE,
                                         in1=biasQ[:].rearrange("p (a c) -> p a c", a=1).to_broadcast([P, NPG, P]),
                                         op0=ALU.mult, op1=ALU.add).then_inc(zS_dve, 1)
                if nxt:
                    t_copy(s + 1, 1)
                dve.wait_ge(zS_dve, 4 * s + 1)
                dve.wait_ge(zS_act, 5 * s + 3)
                dve.scalar_tensor_tensor(out=tlS[:], in0=zbS[:], scalar=0.0, in1=tlS[:], op0=ALU.max, op1=ALU.add
                                         ).then_inc(zS_dve, 1)
                if nxt:
                    t_copy(s + 1, 3)
                dve.wait_ge(zS_dve, 4 * s + 2)
                dve.wait_ge(zS_act, 5 * s + 4)
                dve.tensor_tensor(ulS[:], tlS[:], uhS[:].bitcast(F32), ALU.subtract).then_inc(zS_dve, 1)
                if nxt:
                    t_copy(s + 1, 5)
                dve.wait_ge(RS_full, s + 1)
                dve.tensor_tensor(zbS[:], zbS[:], acc[1][:, 0, :], ALU.subtract).then_inc(zS_dve, 1)
                if nxt:
                    t_copy(s + 1, 7)
                dve.wait_ge(AVS_full, s + 1)
                for hh in range(2):
                    rows = slice(64 * hh, 64 * hh + 64)
                    dve.tensor_copy(attn_o[rows, :, bass.ds(SEQ + NEW * s, NEW)],
                                    pO[rows, 0:P].rearrange("p (j c) -> p j c", c=2 * NEW)[:, :, hh * NEW:(hh + 1) * NEW]
                                    ).then_inc(AVS_free, 1)

            for f in (1, 3, 5, 7):
                t_copy(0, f)
            with dve.Fori(0, NSEQ - 1) as s:
                seq(s, True)
            seq(NSEQ - 1, False)
            dve.wait_ge(AVS_free, 2 * NSEQ + 2)
            for m in range(NB):
                lo_part(xb_lo[:, m, :], xb_hi[:, m, :], attn_o[:, m, :], ao_hi, m + 1)
            add_to_h(U_OB)
            norm_apply(n_norm["mlp1"], n_app["mlp1"], GMLP1, xa_hi, xa_lo)
            mlp(U_MLP1, FCH * NB, xb_hi, xb_lo)
            dve.wait_ge(n_rs, 2 * n_norm["final"] + 2)
            for m in range(NB):
                dve.scalar_tensor_tensor(out=nrm[:, m, :], in0=hT[:, m, :], scalar=gT[:, GFIN + m:GFIN + m + 1],
                                         in1=rstd[:], op0=ALU.mult, op1=ALU.mult).then_inc(n_xf, 1)
            for n in range(SEQ // P + 1):
                w = P if n < SEQ // P else SMP
                dve.wait_ge(y_full, 2 * n + 2)
                dve.wait_ge(y_read, 2 * n + 1)
                if n >= 2:
                    dve.wait_ge(y_stored[n % 2], 16 * (n // 2))
                dve.tensor_copy(yrow[n % 2][0:w, 512:DM], pL[0:w, 1, :]).then_inc(y_read, 1)

        @block.tensor
        def _(pe):
            def unit(s, half, a, U, x_hi, x_lo, Xb):
                unit_part(s, half, a, U, x_hi, x_lo, Xb, 0, 8)

            def unit_part(s, half, a, U, x_hi, x_lo, Xb, k0, k1):
                if k0 == 0:
                    pe.wait_ge(acc_free, U + 1)
                for k in range(k0, k1):
                    if k in (0, 4, 7):
                        pe.wait_ge(x_ready, Xb + {0: 4, 4: 7, 7: 8}[k])
                    for n, (w, x) in enumerate(((whi, x_hi), (whi, x_lo), (wlo, x_hi))):
                        for hf in range(2):
                            last = pe.matmul(acc[a][:, hf, 0:HALF], w[s][:, k, half * P:(half + 1) * P],
                                             x[:, k, hf * HALF:(hf + 1) * HALF], start=(k == 0 and n == 0),
                                             stop=(k == 7 and n == 2))
                if k1 == 8:
                    last.then_inc(unit_done, 1)

            def panel(s, Pn, U, x_hi, x_lo, Xb):
                pe.wait_ge(lo_done, Pn + 1)
                for a in range(2):
                    unit(s, a, a, U + a, x_hi, x_lo, Xb)

            def square(Ub, x_hi, x_lo, Xb):
                with pe.Fori(0, 2) as i:
                    for s in range(2):
                        panel(s, Ub // 2 + 2 * i + s, Ub + 4 * i + 2 * s, x_hi, x_lo, Xb)

            pe.wait_ge(pool_const, 1)
            pe.wait_ge(vec_landed, 96)
            pe.transpose(pO[:, 0:72], vec_rows[:], ident[0:72, 0:72])
            pe.wait_ge(bias_landed, 16)
            pe.matmul(pO[:, 72:72 + H_B], ones[0:1, :], bias_row[:], start=True, stop=True).then_inc(vec_T, 1)
            pe.wait_ge(x_landed, 32)
            for m in range(NB):
                if m >= 2:
                    pe.wait_ge(xT_read, m - 1)
                for c in range(NCH):
                    last = pe.transpose(pL[:, m % 2, c * P:(c + 1) * P], x_rows[:, c, m * P:(m + 1) * P], ident[:])
                last.then_inc(xT_full, 1)
            for m in range(NB):
                last = pe.transpose(pM[:, m * SMP:(m + 1) * SMP], xs_rows[:, m * P:(m + 1) * P], ident[0:SMP, 0:SMP])
            last.then_inc(xT_full, 1)

            def norm_sum(call):
                for m in range(NB):
                    pe.wait_ge(n_sq, NB * call + m + 1)
                    for hf in range(2):
                        last = pe.matmul(pL[:, hf, 0:HALF], ones[:], nrm[:, m, hf * HALF:(hf + 1) * HALF],
                                         start=(m == 0), stop=(m == NB - 1))
                last.then_inc(n_sum, 1)

            pe.wait_ge(xT_read, NB)
            norm_sum(0)

            def head_products(h):
                Lb = 14 * h
                n_lv = len(LEVELS)

                def chunks(t, c):
                    return t[:, c * CH:(c + 1) * CH]

                if not isinstance(h, int) or h:
                    pe.wait_ge(L_free, Lb)
                pe.wait_ge(acc_free, 4 * h + 5)
                for c in range(NCH):
                    last = pe.transpose(pL[:, 0, c * P:(c + 1) * P], chunks(vT, c), ident[:])
                last.then_inc(L_full, 1)
                pe.wait_ge(prep_dve, 4 * h + 4)
                if not isinstance(h, int) or h:
                    pe.wait_ge(M_free, 3 * h)
                for c in range(NCH):
                    last = pe.transpose(pL[:, 1, c * P:(c + 1) * P], chunks(kh, c), ident[:])
                last.then_inc(L_full, 1)
                pe.transpose(pM[0:SMP, 0:P], vT[:, SEQ:T], ident[:])
                pe.transpose(pM[0:SMP, P:2 * P], kh[:, SEQ:T], ident[:]).then_inc(M_full, 1)
                for n in range(n_lv + 1):
                    b = n % 2
                    pe.wait_ge(L_free, Lb + n + 1)
                    if n < n_lv:
                        pe.wait_ge(lev_X, 2 * n_lv * h + 2 * n + 2)
                        lhs, rhs = X[n], X[n]
                    else:
                        lhs, rhs = None, dg
                    if n >= n_lv - SMP_LEVELS:
                        k = n - (n_lv - SMP_LEVELS)
                        last = pe.matmul(pM[0:SMP, 2 * P + k * SMP:2 * P + (k + 1) * SMP],
                                         lhs[:, SEQ:T] if lhs is not None else ones[:, 0:SMP], rhs[:, SEQ:T],
                                         start=True, stop=True)
                        if n == n_lv:
                            last.then_inc(M_full, 1)
                    for c in range(NCH):
                        last = pe.matmul(pL[:, b, c * P:(c + 1) * P], chunks(lhs, c) if lhs is not None else ones[:],
                                         chunks(rhs, c), start=True, stop=True)
                    last.then_inc(L_full, 1)
                pe.wait_ge(L_free, Lb + 9)
                for c in range(NCH):
                    last = pe.matmul(pL[:, 0, c * P:(c + 1) * P], VK[:, 1, c, :], VK[:, 0, c, :], start=True, stop=True)
                last.then_inc(L_full, 1)
                pe.wait_ge(vblk_ready, h + 1)
                for n in range(2):
                    pe.wait_ge(L_free, Lb + 10 + n)
                    pe.matmul(pL[:, (n + 1) % 2, :], VK[0:SMP, 1, NCH, :],
                              Vblk[:, 4 * n:4 * n + 4, :].rearrange("p s v -> p (s v)"), start=True, stop=True
                              ).then_inc(L_full, 1)
                pe.wait_ge(L_free, Lb + 11)
                if not isinstance(h, int) or h:
                    pe.wait_ge(o_norm, h)
                for c in range(NCH):
                    last = pe.matmul(pO[:, c * P:(c + 1) * P], VK[:, 0, c, :], Amat[:, c, :], start=True, stop=(c == 0))
                    if c:
                        last = pe.matmul(pO[:, c * P:(c + 1) * P], S[:, c - 1, :], chunks(qe, c), start=False, stop=True)
                last.then_inc(o_full, 1)
                pe.wait_ge(M_free, 3 * h + 2)
                pe.wait_ge(s0_landed, 16 * h + 16)
                pe.matmul(pM[:, 0:SMP], VK[0:SMP, 0, NCH, :], As[:], start=True, stop=False)
                for s in range(NSEQ):
                    last = pe.matmul(pM[:, s * NEW:(s + 1) * NEW], S0[:, s, :], qe[:, SEQ + s * NEW:SEQ + (s + 1) * NEW],
                                     start=False, stop=(s == NSEQ - 1))
                last.then_inc(M_full, 1)
                pe.wait_ge(o_sq, 2 * h + 1)
                pe.wait_ge(L_free, Lb + 12)
                pe.matmul(pL[:, 1, :], ones[:], t1[:, 0:SEQ], start=True, stop=True).then_inc(L_full, 1)
                pe.wait_ge(o_sq, 2 * h + 2)
                pe.matmul(pM[:, SMP:2 * SMP], ones[:], t1[:, SEQ:T], start=True, stop=True).then_inc(M_full, 1)

            panel(0, 0, 0, xa_hi, xa_lo, X_N0)
            panel(1, 1, 2, xa_hi, xa_lo, X_N0)
            panel(0, 2, 4, xa_hi, xa_lo, X_N0)
            head_products(0)
            panel(1, 3, 6, xa_hi, xa_lo, X_N0)
            with pe.Fori(2, NB) as h:
                panel(0, 2 * h, 4 * h, xa_hi, xa_lo, X_N0)
                head_products(h - 1)
                panel(1, 2 * h + 1, 4 * h + 2, xa_hi, xa_lo, X_N0)
            head_products(NB - 1)
            square(U_OUT, xa_hi, xa_lo, X_HG)

            def mlp(Ub, Xn, X0, x_hi, x_lo, h_hi, h_lo):
                with pe.Fori(0, FCH) as c:
                    with pe.Fori(0, 2) as i:
                        for s in range(2):
                            panel(s, Ub // 2 + 8 * c + 2 * i + s, Ub + 16 * c + 4 * i + 2 * s, x_hi, x_lo, Xn)
                    with pe.Fori(0, 2) as i:
                        for s in range(2):
                            panel(s, Ub // 2 + 4 + 8 * c + 2 * i + s, Ub + 8 + 16 * c + 4 * i + 2 * s, h_hi, h_lo,
                                  X0 + NB * c)

            norm_sum(n_norm["mlp0"])
            mlp(U_MLP0, X_N1, X_HID0, xa_hi, xa_lo, xb_hi, xb_lo)
            norm_sum(n_norm["mix1"])
            square(U_Q, xa_hi, xa_lo, X_Q)

            def logits(j, n):
                hh, g = divmod(n, 3)
                rows = slice(64 * hh, 64 * hh + 64)
                pe.wait_ge(B_free, 8 * j + n + 3)
                if n == 0:
                    pe.wait_ge(kq_lo, 2 * j + 2)
                for kb, c0 in GROUPS[g]:
                    w = SEQ - kb * P
                    for m, (k, q) in enumerate(((khi, qhi), (khi, qlo), (klo, qhi))):
                        pe.matmul(pL[:, n % 2, c0:c0 + w], k[rows, kb * P:(kb + 1) * P], q[rows, kb * P:SEQ],
                                  start=(m == 0), stop=False)
                    last = pe.matmul(pL[:, n % 2, c0:c0 + P], ident_r[:], neg_r[:], start=False, stop=True)
                last.then_inc(B_full, 1)

            def later_sums(j, n):
                hh, g = divmod(n, 3)
                pe.wait_ge(la_done, 6 * j + n + 1)
                if n == 0:
                    pe.wait_ge(R_free, j + 1)
                pe.wait_ge(u_lo, 6 * j + n + 1)
                for kb, c0 in GROUPS[g]:
                    for k2 in range(kb, NCH):
                        w = SEQ - k2 * P
                        c = c0 + (k2 - kb) * P
                        for u in (uh[hh], ul[hh]):
                            last = pe.matmul(pM[:, c:c + w], (tri_r if k2 == kb else ones_r)[:],
                                             u[:, UOFF[k2]:UOFF[k2] + w], start=(k2 == kb and u is uh[hh]),
                                             stop=(k2 == NCH - 1 and u is ul[hh]))
                last.then_inc(R_full, 1)

            def weighted(j, hh):
                pe.wait_ge(AV_free, 2 * j + hh + 1)
                pe.wait_ge(a_done, 6 * j + 3 * hh + 5)
                for kb in range(NCH):
                    w = SEQ - kb * P
                    last = pe.matmul(pO[:, kb * P:SEQ], vr[:, kb, :], Am[:, UOFF[kb]:UOFF[kb] + w], start=(kb == 0),
                                     stop=(kb == NCH - 1))
                last.then_inc(AV_full, 1)

            def pair(j, par, nxt):
                s = 1 - par
                U = U_KV + 2 * j
                for n, t in enumerate((kf, vf)):
                    if n == 1:
                        pe.wait_ge(la_done, 6 * j + 1)
                    pe.wait_ge(acc_free, U + n + 3)
                    pe.wait_ge(B_free, 8 * j + n + 1)
                    for c in range(NCH):
                        last = pe.transpose(pL[:, n, c * P:(c + 1) * P], t[:, c * P:(c + 1) * P], ident[:])
                    last.then_inc(B_full, 1)
                pe.transpose(pM[0:SMP, 0:P], kf[:, SEQ:T], ident[:])
                pe.transpose(pM[0:SMP, P:2 * P], vf[:, SEQ:T], ident[:]).then_inc(R_full, 1)

                def fill(a, k0, k1):
                    if nxt:
                        if a == 0 and k0 == 0:
                            pe.wait_ge(lo_done, U_KV // 2 + j + 2)
                        unit_part(s, a, a, U + 2 + a, xb_hi, xb_lo, X_KV, k0, k1)

                logits(j, 0)
                logits(j, 1)
                fill(0, 0, 3)
                later_sums(j, 0)
                logits(j, 2)
                fill(0, 3, 6)
                later_sums(j, 1)
                logits(j, 3)
                fill(0, 6, 8)
                later_sums(j, 2)
                logits(j, 4)
                fill(1, 0, 3)
                weighted(j, 0)
                later_sums(j, 3)
                logits(j, 5)
                fill(1, 3, 6)
                later_sums(j, 4)
                fill(1, 6, 8)
                later_sums(j, 5)
                weighted(j, 1)

            panel(0, U_KV // 2, U_KV, xb_hi, xb_lo, X_KV)
            with pe.Fori(0, NPAIR // 2 - 1) as i:
                for par in range(2):
                    pair(2 * i + par, par, True)
            pair(NPAIR - 2, 0, True)
            pair(NPAIR - 1, 1, False)

            pe.wait_ge(la_done, 6 * NPAIR + 1)
            pe.wait_ge(kts_done, NPAIR)
            for h in range(H_B):
                rows = slice(64 * (h % 2), 64 * (h % 2) + 64)
                last = pe.matmul(pL[0:SMP, h % 2, (h // 2) * SMP:(h // 2 + 1) * SMP], kTs[rows, h // 2, :],
                                 qT[rows, h // 2, SEQ:T], start=True, stop=True)
            last.then_inc(new_full, 1)
            pe.wait_ge(new_dve, 4)
            for n in range(2):
                for u in (uhN, ulN):
                    last = pe.matmul(pL[:, n, :], tri_r[0:SMP, :], u[:, 8 * n:8 * n + 8, :].rearrange(
                        "p h t -> p (h t)"), start=(u is uhN), stop=(u is ulN))
            last.then_inc(new_full, 1)

            def t_fill(s, b, f, nth):
                if f == 0:
                    pe.wait_ge(kp_landed[b], 64 * nth)
                free = (Ta_free, Td_free)[f % 2]
                if f >= 4:
                    pe.wait_ge(free, 4 * s + (f - 4) // 2 + 1)
                elif not isinstance(s, int) or s:
                    pe.wait_ge(free, 4 * s + f // 2 - 1)
                for p in range(4):
                    j = 4 * (f % 2) + p
                    last = pe.transpose(T_bank(f)[:, p * P:(p + 1) * P], Kp[b][:, f // 2, j * P:(j + 1) * P], ident[:])
                last.then_inc(T_full, 1)

            def seq(s, b, i, nxt):
                pe.wait_ge(Ta_free, 4 * s + 4)
                pe.wait_ge(Td_free, 4 * s + 4)
                for g in range(NPG):
                    for j in range(NPAIR):
                        c = g * P + j * 2 * NEW
                        last = pe.matmul(pM[:, c:c + 2 * NEW], KT[:, j, g, :], qblk[:, j, bass.ds(s, 1), :].rearrange(
                            "p a n -> p (a n)"), start=True, stop=True)
                last.then_inc(zS_full, 1)
                if nxt:
                    for f in range(6):
                        t_fill(s + 1, 1 - b, f, i + 1 + b)
                pe.wait_ge(zS_dve, 4 * s + 3)
                rS = acc[1][:, 0, :]
                for g in range(NPG):
                    for g2 in range(g, NPG):
                        for u in (uhS, ulS):
                            pe.matmul(rS[:, g * P:(g + 1) * P], (tri_r if g2 == g else ones_r)[:],
                                      u[:, g2 * P:(g2 + 1) * P], start=(g2 == g and u is uhS), stop=False)
                    for u in (uhN, ulN):
                        last = pe.matmul(rS[:, g * P:(g + 1) * P], ones_r[0:SMP, :],
                                         u[:, :, bass.ds(NEW * s, NEW)], start=False, stop=(u is ulN))
                last.then_inc(RS_full, 1)
                if nxt:
                    for f in range(6, 8):
                        t_fill(s + 1, 1 - b, f, i + 1 + b)
                pe.wait_ge(vp_landed[b], 64 * i + 64)
                pe.wait_ge(AVS_free, 2 * s + 2)
                pe.wait_ge(zS_act, 5 * s + 5)
                for j in range(NPAIR):
                    c = j * 2 * NEW
                    for g in range(NPG):
                        pe.matmul(pO[:, c:c + 2 * NEW], Vp[b][:, g, j * P:(j + 1) * P],
                                  AS[:, g * P + c:g * P + c + 2 * NEW], start=(g == 0), stop=False)
                    last = pe.matmul(pO[:, c:c + 2 * NEW], kvn[:, 1, j, :], AN[:, 2 * j:2 * j + 2, bass.ds(NEW * s, NEW)],
                                     start=False, stop=True)
                last.then_inc(AVS_full, 1)

            pe.wait_ge(new_dve, 5)
            pe.wait_ge(new_act, 5)
            for f in range(8):
                t_fill(0, 0, f, 1)
            with pe.Fori(0, NSEQ // 2 - 1) as i:
                for b in range(2):
                    seq(2 * i + b, b, i, True)
            seq(NSEQ - 2, 0, NSEQ // 2 - 1, True)
            seq(NSEQ - 1, 1, NSEQ // 2 - 1, False)
            square(U_OB, xb_hi, xb_lo, X_OB)
            norm_sum(n_norm["mlp1"])
            mlp(U_MLP1, X_N3, X_HID1, xa_hi, xa_lo, xb_hi, xb_lo)
            norm_sum(n_norm["final"])
            for n in range(SEQ // P + 1):
                w = P if n < SEQ // P else SMP
                for hf in range(2):
                    pe.wait_ge(n_xf, NB * n_app["final"] + 4 * hf + 4)
                    if n:
                        pe.wait_ge(y_read, 2 * n - 1 + hf)
                    for m in range(4):
                        last = pe.transpose(pL[0:w, hf, m * P:(m + 1) * P], nrm[:, 4 * hf + m, n * P:n * P + w], ident[:])
                    last.then_inc(y_full, 1)


_INS = ["x_prompt", "x_sample", "state_hgrn", "cache_k", "cache_v", "page_table", "lb_logits", "w_in_a", "g_onorm_a",
        "w_out_a", "w_kv", "g_kv", "w_q_b", "w_out_b", "sb_bias", "w_up", "w_down", "g_mix", "g_mlp", "g_final"]
_OUTS = [(1, SEQ, DM), (NSEQ, NEW, DM), (1, 1, NB, P, P), (1, NSEQ, NB, P, P), (1, SEQ, H_B, HD), (1, SEQ, H_B, HD),
         (NSEQ, NEW, H_B, HD), (NSEQ, NEW, H_B, HD)]


def kernel(**inputs):
    import numpy as _np
    import concourse.bacc as _bacc
    from concourse import mybir as _mybir
    from concourse.bass_utils import run_bass_kernel_spmd as _run

    nc = _bacc.Bacc("TRN2", target_bir_lowering=False, num_devices=1)
    arrays, args = {}, []
    for name in _INS:
        a = _np.ascontiguousarray(inputs[name])
        arrays[f"in_{name}_dram"] = a
        args.append(nc.dram_tensor(f"in_{name}_dram", a.shape, _mybir.dt.from_np(a.dtype), kind="ExternalInput").ap())
    for i, shape in enumerate(_OUTS):
        args.append(nc.dram_tensor(f"out_{i}_dram", shape, F32, kind="ExternalOutput").ap())
    yoco_step(nc, *args)
    r = _run(nc, [arrays], core_ids=[0])
    return tuple(r.results[0][f"out_{i}_dram"] for i in range(len(_OUTS)))
```

```python
from contextlib import ExitStack

import concourse.bass as bass
from concourse import mybir
from concourse.alu_op_type import AluOpType as ALU

ACT = mybir.ActivationFunctionType
F32 = mybir.dt.float32
F32R = mybir.dt.float32r
U32 = mybir.dt.uint32
I32 = mybir.dt.int32

P = 128
DM = 1024
NB = DM // P
SEQ = 512
NSEQ = 8
NEW = 8
SMP = NSEQ * NEW
T = SEQ + SMP
HALF = T // 2
CH = 128
NCH = SEQ // CH
H_B = 16
HD = DM // H_B
NPAIR = H_B // 2
PAGE = 128
NPG = 4
FCH = 4
EPS = 1e-6
CLAMP = -43.0
NEG = -1e30
SCALE = HD ** -0.5
LEVELS = [64, 32, 16, 8, 4, 2, 1]
SMP_LEVELS = 3

LB0, LB1, GON, GKV, GMIX0, GMIX1, GMLP0, GMLP1, GFIN = range(0, 72, 8)


class Count:

    def __init__(self, sem, base=0, i=0, per=0):
        self.sem, self.base, self.i, self.per, self.k = sem, base, i, per, 0

    def inc(self, ins):
        ins.then_inc(self.sem, 1)
        self.k += 1
        return self.at(self.k)

    def at(self, k):
        return self.base + self.i * self.per + k if self.per else self.base + k

    def end(self):
        assert self.k == self.per, (self.k, self.per)


def yoco_step(nc, x_prompt, x_sample, state_hgrn, cache_k, cache_v, page_table, lb_logits, w_in_a,
              g_onorm_a, w_out_a, w_kv, g_kv, w_q_b, w_out_b, sb_bias, w_up, w_down, g_mix, g_mlp,
              g_final, y_prompt, y_sample, st_prompt, st_sample, k_prompt, v_prompt, k_sample, v_sample):
    ctx = ExitStack()
    with ctx:
        top = [nc.sbuf_base + (-nc.sbuf_base) % 64]
        limit = nc.sbuf_usable_end

        def sb_at(name, shape, dt, offset):
            n = 4
            for d in shape[1:]:
                n *= d
            assert offset + n <= limit, (name, offset + n, limit)
            return nc.alloc_sbuf_tensor_at(name, shape, dt, offset=offset), offset + (n + 63) // 64 * 64

        def sb(name, shape, dt=F32):
            t, top[0] = sb_at(name, shape, dt, top[0])
            return t

        def arena(start, items):
            out = []
            for name, shape, dt in items:
                t, start = sb_at(name, shape, dt, start)
                out.append(t)
            return out

        ident = sb("ident", [P, P])
        ones = sb("ones", [P, P])
        ones_r = sb("ones_r", [P, P], F32R)
        tri_r = sb("tri_r", [P, P], F32R)
        ident_r = sb("ident_r", [P, P], F32R)
        gT = sb("gT", [P, 72])
        lb = sb("lb", [P, NB])
        omlb = sb("omlb", [P, NB])
        bias_h = sb("bias_h", [P, H_B])
        eps_t = sb("eps_t", [P, 1])
        small = sb("small", [P, 4 * NB])
        wait_mark = sb("wait_mark", [1, 16])
        start_mark = sb("start_mark", [1, 16])
        neg_r = sb("neg_r", [P, P], F32R)
        neg_s = sb("neg_s", [SMP, SMP])
        row_head = sb("row_head", [P, H_B])
        row_pair = sb("row_pair", [P, NPAIR])
        row_bias = sb("row_bias", [P, 1])
        bias_m = sb("bias_m", [P, H_B])
        newR = sb("newR", [P, NSEQ])
        pt = sb("pt", [1, NSEQ * NPG], I32)
        rstd = sb("rstd", [P, T])
        hT = sb("hT", [P, NB, T])
        wraw = [sb(f"wraw{s}", [P, 8, 256]) for s in range(2)]
        whi = [sb(f"whi{s}", [P, 8, 256], F32R) for s in range(2)]
        wlo = [sb(f"wlo{s}", [P, 8, 256], F32R) for s in range(2)]
        xa_at = top[0]
        xa_hi = sb("xa_hi", [P, NB, T], F32R)
        xa_lo = sb("xa_lo", [P, NB, T], F32R)
        xb_at = top[0]
        xb_hi = sb("xb_hi", [P, NB, T], F32R)
        xb_lo = sb("xb_lo", [P, NB, T], F32R)
        ar = top[0]


        tri_f, neg_f = arena(xb_at + NB * T * 4 + T * 4, [("tri_f", [P, P], F32), ("neg_f", [P, P], F32)])
        xc_at = xb_at + NB * T * 4
        xe_at = xa_at + NB * T * 4
        hgrn_o = sb_at("hgrn_o", [P, NB, T], F32, xb_at)[0]
        attn_o = sb_at("attn_o", [P, NB, T], F32, xa_at)[0]
        x_rows, xs_rows = arena(xb_at, [("x_rows", [P, SEQ // P, DM], F32), ("xs_rows", [SMP, DM], F32)])
        vec_rows, bias_row = arena(xa_at, [("vec_rows", [72, P], F32), ("bias_row", [1, H_B], F32)])
        TW = [SEQ] * (len(LEVELS) - SMP_LEVELS) + [T] * SMP_LEVELS
        masks, scan_keep, seqmask = arena(ar, [("masks", [P, len(LEVELS), P], F32), ("scan_keep", [P, T], F32),
                                               ("seqmask", [SMP, NSEQ], F32)])
        ar1 = ar + 4 * (len(LEVELS) * P + T) + 64
        (cl0, qq, t1, t2, fg, kk, G, tq, sgg, vT, eG, ek, kh, qe, dg, S, Amat, As, VK, *X) = arena(
            ar1, [(n, [P, T], F32) for n in ["cl0", "qq", "t1", "t2", "fg", "kk", "G", "tq", "sgg", "vT", "eG", "ek",
                                             "kh", "qe", "dg"]]
            + [("S", [P, NCH, P], F32), ("Amat", [P, NCH, P], F32), ("As", [SMP, SMP], F32), ("VK", [P, 2, 5, P], F32)]
            + [(f"X{n}", [P, w], F32) for n, w in enumerate(TW[:-1])])
        D0, D1, S0, Sn, X_last = arena(xc_at, [("D0", [P, T], F32), ("D1", [P, T], F32), ("S0", [P, NSEQ, P], F32),
                                               ("Sn", [P, NSEQ, P], F32), ("X_last", [P, T], F32)])
        X.append(X_last)
        D = [D0, D1]
        (Vblk,) = arena(ar1 + 15 * T * 4 + 2 * 2048 + 256 + 5120, [("Vblk", [SMP, NSEQ, P], F32)])
        GROUPS = [[(3, 0), (2, 128)], [(1, 0)], [(0, 0)]]
        GCOL, GW = [0, 384, 768], [384, 384, 512]
        UOFF = {3: 0, 2: 128, 1: 384, 0: 768}
        qT_at = (limit - NB * T * 4) // 64 * 64
        (qT,) = arena(qT_at, [("qT", [P, NB, T], F32)])
        (kf, vf, khi, klo, qhi, qlo, kr, vr, uh0, ul0, Am, zb0, zb1, tl0, tl1, ul1) = arena(
            ar, [("kf", [P, T], F32), ("vf", [P, T], F32), ("khi", [P, T], F32R), ("klo", [P, T], F32R),
                 ("qhi", [P, SEQ], F32R), ("qlo", [P, SEQ], F32R), ("kr", [P, NCH, P], F32), ("vr", [P, NCH, P], F32),
                 ("uh0", [P, 1280], F32R), ("ul0", [P, 1280], F32R), ("Am", [P, 1280], F32), ("zb0", [P, 512], F32),
                 ("zb1", [P, 512], F32), ("tl0", [P, 512], F32), ("tl1", [P, 512], F32), ("ul1", [P, 1280], F32R)])
        kTs, kvn, uh1 = arena(xe_at, [("kTs", [P, NPAIR, SMP], F32), ("kvn", [SMP, 2, NPAIR, P], F32),
                                      ("uh1", [P, 1280], F32R)])
        uh, ul, zb, tl = [uh0, uh1], [ul0, ul1], [zb0, zb1], [tl0, tl1]
        uhN, ulN = arena(xe_at + 2048 + 8192, [("uhN", [SMP, H_B, SMP], F32R), ("ulN", [SMP, H_B, SMP], F32R)])
        (AN,) = arena(xe_at + 2048, [("AN", [SMP, H_B, SMP], F32)])
        Kp0, Kp1 = arena(xb_at, [(f"Kp{n}", [P, NPG, DM], F32) for n in range(2)])
        (QB0, QB1, qTs, Oc, AN0, AN1, Vp0, Vp1, KT) = arena(
            ar, [("QB0", [P, NPAIR, P + 2 * NEW], F32), ("QB1", [P, NPAIR, P + 2 * NEW], F32),
                 ("qTs", [P, NPAIR, SMP], F32), ("Oc", [P, P], F32), ("AN0", [SMP, P], F32), ("AN1", [SMP, P], F32),
                 ("Vp0", [P, NPG, DM], F32), ("Vp1", [P, NPG, DM], F32), ("KT", [P, NPAIR, NPG, P], F32)])
        (zbS,) = arena(xe_at, [("zbS", [P, 512], F32)])
        tlS, RS, AS, AT = arena(xe_at + 2048 + 8192, [("tlS", [P, 512], F32), ("RS", [P, 512], F32),
                                                      ("AS", [P, 512], F32), ("AT", [P, NPG, P], F32)])
        (O_m,) = arena(xb_at + 2 * NPG * DM * 4, [("O_m", [P, NPAIR, P], F32)])
        QB, ANs = [QB0, QB1], [AN0, AN1]
        Kp, Vp = [Kp0, Kp1], [Vp0, Vp1]
        zbN, tlN, biasN, tlNs = arena(ar + 12800, [("zbN", [SMP, H_B, SMP], F32), ("tlN", [SMP, H_B, SMP], F32),
                                             ("biasN", [SMP, H_B, SMP], F32), ("tlNs", [SMP, NSEQ, P], F32)])
        yrow0, yrow1 = arena(xb_at, [("yrow0", [P, DM], F32), ("yrow1", [P, DM], F32)])
        yrow = [yrow0, yrow1]
        nrm, *mlp_t = arena(ar1, [("nrm", [P, NB, T], F32)] + [(f"mlp{i}", [P, T], F32) for i in range(4)])
        relu_t, sqr_t = mlp_t[:2], mlp_t[2:]

        def ps(name, shape):
            return ctx.enter_context(nc.psum_tensor(name, shape, F32))

        acc = [ps(f"acc{s}", [P, 2, 512]) for s in range(2)]
        pL = ps("pL", [P, 2, 512])
        pM = ps("pM", [P, 512])
        pO = ps("pO", [P, 512])

        def T_bank(f):
            return (pL[:, 0, :], pL[:, 1, :], acc[0][:, 0, :], acc[0][:, 1, :])[f % 4]

        def sem(name):
            return ctx.enter_context(nc.semaphore(name))

        raw_landed = [sem(f"raw_landed{s}") for s in range(2)]
        hi_done = sem("hi_done")
        lo_done = sem("lo_done")
        unit_done = sem("unit_done")
        acc_free = sem("acc_free")
        x_ready = sem("x_ready")
        vec_landed = sem("vec_landed")
        bias_landed = sem("bias_landed")
        x_landed = sem("x_landed")
        pool_const = sem("pool_const")
        pool_chain = sem("pool_chain")
        dve_const = sem("dve_const")
        act_const = sem("act_const")
        vec_T = sem("vec_T")
        lbs = sem("lbs")
        lbs_act = sem("lbs_act")
        xT_full = sem("xT_full")
        xT_read = sem("xT_read")
        n_sq, n_tot, n_sum, n_rs, n_xf, n_hi = (sem(n) for n in ("n_sq", "n_tot", "n_sum", "n_rs", "n_xf", "n_hi"))
        fz_act, fz_dve, q_act, q_dve, og_act, og_dve = (sem(n) for n in ("fz_act", "fz_dve", "q_act", "q_dve",
                                                                         "og_act", "og_dve"))
        prep_act, prep_dve, lev_D, lev_E, lev_X = (sem(n) for n in ("prep_act", "prep_dve", "lev_D", "lev_E", "lev_X"))
        L_full, L_free, M_full, M_free = (sem(n) for n in ("L_full", "L_free", "M_full", "M_free"))
        as_chain, vblk_ready, s_chain, sn_scaled = (sem(n) for n in ("as_chain", "vblk_ready", "s_chain", "sn_scaled"))
        o_full, o_sq, o_rs, o_norm, o_out = (sem(n) for n in ("o_full", "o_sq", "o_rs", "o_norm", "o_out"))
        s0_landed, state_stored = sem("s0_landed"), sem("state_stored")
        sqr_done, hid_hi = sem("sqr_done"), sem("hid_hi")
        ho_hi = sem("ho_hi")
        y_full, y_read = sem("y_full"), sem("y_read")
        y_stored = [sem(f"y_stored{n}") for n in range(2)]

        tri_done = sem("tri_done")
        pt_landed = sem("pt_landed")
        B_full, B_free, R_full, R_free, AV_full, AV_free = (sem(n) for n in ("B_full", "B_free", "R_full", "R_free",
                                                                             "AV_full", "AV_free"))
        k_hi, kq_lo, q_hi, soft, sp_done, u_hi, u_lo, la_done, a_done = (sem(n) for n in (
            "k_hi", "kq_lo", "q_hi", "soft", "sp_done", "u_hi", "u_lo", "la_done", "a_done"))
        new_chain = sem("new_chain")
        kts_done, kv_stored = sem("kts_done"), sem("kv_stored")
        new_full, new_dve, new_act, qblk_done = (sem(n) for n in ("new_full", "new_dve", "new_act", "qblk_done"))
        kp_landed = [sem(f"kp_landed{n}") for n in range(2)]
        vp_landed = [sem(f"vp_landed{n}") for n in range(2)]
        T_full, Ta_free, Td_free = sem("T_full"), sem("Ta_free"), sem("Td_free")
        zS_full, zS_dve, zS_act, AT_full, O_full, O_dve, fin_full, fin_free = (sem(n) for n in (
            "zS_full", "zS_dve", "zS_act", "AT_full", "O_full", "O_dve", "fin_full", "fin_free"))
        QB_ready, ANs_ready = sem("QB_ready"), sem("ANs_ready")
        ao_hi = sem("ao_hi")

        block = ctx.enter_context(nc.Block())

        U_IN, U_OUT, U_MLP0 = 0, 4 * NB, 5 * NB
        U_Q = U_MLP0 + 2 * FCH * NB
        U_KV = U_Q + NB
        U_OB = U_KV + 2 * NB
        U_MLP1 = U_OB + NB
        U_END = U_MLP1 + 2 * FCH * NB
        X_N0, X_HG, X_N1 = 0, NB, 2 * NB
        X_HID0 = 3 * NB
        X_Q = X_HID0 + FCH * NB
        X_KV = X_Q + NB
        X_OB = X_KV + NB
        X_N3 = X_OB + NB
        X_HID1 = X_N3 + NB
        n_norm = {"mix0": 0, "mlp0": 1, "mix1": 2, "mlp1": 3, "final": 4}
        n_app = {"mix0": 0, "mlp0": 1, "q": 2, "kv": 3, "mlp1": 4, "final": 5}

        w_in_v = w_in_a.rearrange("l (k p) (g n) -> p (l k) g n", p=P, g=4)
        w_out_v = w_out_a.rearrange("l (k p) n -> p (l k) n", p=P)
        w_kv_v = w_kv.rearrange("(k p) (g n) -> p k g n", p=P, g=2)
        w_q_v = w_q_b.rearrange("l (k p) n -> p (l k) n", p=P)
        w_ob_v = w_out_b.rearrange("l (k p) n -> p (l k) n", p=P)
        w_up_v = [w_up[n].rearrange("(k p) n -> p k n", p=P) for n in range(2)]
        w_down_v = [w_down[n].rearrange("(c k p) n -> p c k n", p=P, k=8) for n in range(2)]
        k_out = k_prompt.rearrange("a (c p) h d -> p (a c) (h d)", p=P)
        v_out = v_prompt.rearrange("a (c p) h d -> p (a c) (h d)", p=P)
        tok2 = "p (a b) -> p a b"

        @block.sync
        def _(sp):
            def panel(s, Pn, halves, first=False):
                if not first:
                    sp.wait_ge(lo_done, Pn - 1)
                for dst, src in halves:
                    sp.dma_start(dst, src).then_inc(raw_landed[s], 16)

            def plain(s, w, col):
                return [(wraw[s][:, 4 * q:4 * q + 4, :], w(q)[:, :, bass.ds(col, 256)]) for q in range(2)]

            def w_in_halves(s, h):
                parts = [(1, 0), (2, 3)][s]
                return [(wraw[s][:, :, n * P:(n + 1) * P], w_in_v[:, :, part, bass.ts(h, P)])
                        for n, part in enumerate(parts)]

            def square(Pb, w):
                with sp.Fori(0, 2) as i:
                    for s in range(2):
                        panel(s, Pb + 2 * i + s, plain(s, w, 512 * i + 256 * s))

            for s in range(2):
                panel(s, s, w_in_halves(s, 0), first=True)
            with sp.Fori(1, NB) as h:
                for s in range(2):
                    panel(s, 2 * h + s, w_in_halves(s, h))
            square(U_OUT // 2, lambda q: w_out_v[:, 4 * q:4 * q + 4, :])

            def mlp(n, Ub):
                with sp.Fori(0, FCH) as c:
                    with sp.Fori(0, 2) as i:
                        for s in range(2):
                            panel(s, Ub // 2 + 8 * c + 2 * i + s,
                                  plain(s, lambda q: w_up_v[n][:, 4 * q:4 * q + 4, :], 1024 * c + 512 * i + 256 * s))
                    with sp.Fori(0, 2) as i:
                        for s in range(2):
                            panel(s, Ub // 2 + 4 + 8 * c + 2 * i + s,
                                  plain(s, lambda q: w_down_v[n][:, bass.ds(c, 1), 4 * q:4 * q + 4, :].rearrange(
                                      "p c k n -> p (c k) n"), 512 * i + 256 * s))

            mlp(0, U_MLP0)
            square(U_Q // 2, lambda q: w_q_v[:, 4 * q:4 * q + 4, :])
            with sp.Fori(0, NPAIR // 2) as i:
                for s in range(2):
                    panel(s, U_KV // 2 + 2 * i + s,
                          [(wraw[s][:, :, n * P:(n + 1) * P], w_kv_v[:, :, n, bass.ds(256 * i + 128 * s, P)])
                           for n in range(2)])
            sp.dma_start(pt[:], page_table.rearrange("s g -> (s g)").rearrange("(a n) -> a n", a=1)).then_inc(pt_landed, 16)
            sp.wait_ge(pt_landed, 16)

            def key_pages(s, b, first):
                for g in range(NPG):
                    page = sp.value_load(pt[0:1, bass.ds(4 * s + g, 1)], min_val=0, max_val=cache_k.shape[0] - 1)
                    if g == 0 and not first:
                        sp.wait_ge(zS_full, s - 1)
                    sp.dma_start(Kp[b][:, g, :], cache_k[bass.ds(page, 1)].rearrange("a p h d -> p (a h d)")
                                 ).then_inc(kp_landed[b], 16)

            def value_pages(s, b, first):
                for g in range(NPG):
                    page = sp.value_load(pt[0:1, bass.ds(4 * s + g, 1)], min_val=0, max_val=cache_k.shape[0] - 1)
                    if g == 0 and not first:
                        sp.wait_ge(O_full, s - 1)
                    sp.dma_start(Vp[b][:, g, :], cache_v[bass.ds(page, 1)].rearrange("a p h d -> p (a h d)")
                                 ).then_inc(vp_landed[b], 16)

            for s in range(2):
                panel(s, U_OB // 2 + s, plain(s, lambda q: w_ob_v[:, 4 * q:4 * q + 4, :], 256 * s))
            sp.wait_ge(unit_done, U_OB)
            for s in range(2):
                key_pages(s, s, True)
            sp.wait_ge(AV_free, 2 * NPAIR + 1)
            sp.wait_ge(qblk_done, 4)
            for s in range(2):
                value_pages(s, s, True)
            with sp.Fori(1, NSEQ // 2) as i:
                for b in range(2):
                    key_pages(2 * i + b, b, False)
                    value_pages(2 * i + b, b, False)
            for s in range(2):
                panel(s, U_OB // 2 + 2 + s, plain(s, lambda q: w_ob_v[:, 4 * q:4 * q + 4, :], 512 + 256 * s))
            mlp(1, U_MLP1)
            for n in range(SEQ // P + 1):
                sp.wait_ge(y_read, 2 * n + 2)
                if n < SEQ // P:
                    sp.dma_start(y_prompt[0, n * P:(n + 1) * P, :], yrow[n % 2][:]).then_inc(y_stored[n % 2], 16)
                else:
                    sp.dma_start(y_sample.rearrange("s n d -> (s n) d"), yrow[n % 2][0:SMP, :]).then_inc(y_stored[n % 2], 16)
            sp.wait_ge(y_stored[0], 48)
            sp.wait_ge(y_stored[1], 32)
            sp.wait_ge(kv_stored, 32 * NPAIR + 32)
            sp.wait_ge(state_stored, 32 * NB)

        @block.gpsimd
        def _(pool):
            chain = Count(pool_chain)

            def link(ins):
                pool.wait_ge(pool_chain, chain.inc(ins))

            link(pool.memset(ident[:], 0.0))
            link(pool.affine_select(out=ident[:], in_=ident[:], compare_op=ALU.not_equal, fill=1.0, base=0,
                                    pattern=[[-1, P]], channel_multiplier=1))
            pool.memset(ones[:], 1.0).then_inc(pool_const, 1)
            link(pool.memset(masks[:], 0.0))
            for n, m in enumerate(LEVELS):
                link(pool.memset(masks[:, n, :].rearrange("p (b j) -> p b j", j=2 * m)[:, :, m:2 * m], 1.0))
            for n, m in enumerate(LEVELS):
                nb = P // (2 * m)
                v = masks[:, n, :].rearrange("p (b j) -> p b j", j=2 * m)
                link(pool.affine_select(out=v, in_=v, compare_op=ALU.is_ge, fill=0.0, base=0,
                                        pattern=[[-2 * m, nb], [0, 2 * m]], channel_multiplier=1))
                link(pool.affine_select(out=v, in_=v, compare_op=ALU.is_ge, fill=0.0, base=m - 1,
                                        pattern=[[2 * m, nb], [0, 2 * m]], channel_multiplier=-1))
            link(pool.memset(scan_keep[:], 1.0))
            link(pool.memset(scan_keep[:, 0:SEQ:CH], 0.0))
            link(pool.memset(scan_keep[:, SEQ:T:NEW], 0.0))
            link(pool.memset(seqmask[:], 1.0))
            link(pool.affine_select(out=seqmask[:], in_=seqmask[:], compare_op=ALU.is_ge, fill=0.0, base=0,
                                    pattern=[[-NEW, NSEQ]], channel_multiplier=1))
            pool.affine_select(out=seqmask[:], in_=seqmask[:], compare_op=ALU.is_ge, fill=0.0, base=NEW - 1,
                               pattern=[[NEW, NSEQ]], channel_multiplier=-1).then_inc(pool_const, 1)
            for t, w, n in ((row_head, NEW, H_B), (row_pair, 2 * NEW, NPAIR)):
                link(pool.memset(t[:], 1.0))
                link(pool.affine_select(out=t[:], in_=t[:], compare_op=ALU.is_ge, fill=0.0, base=0,
                                        pattern=[[-w, n]], channel_multiplier=1))
                link(pool.affine_select(out=t[:], in_=t[:], compare_op=ALU.is_ge, fill=0.0, base=w - 1,
                                        pattern=[[w, n]], channel_multiplier=-1))
            link(pool.memset(tri_f[:], 1.0))
            link(pool.affine_select(out=tri_f[:], in_=tri_f[:], compare_op=ALU.is_ge, fill=0.0, base=0,
                                    pattern=[[-1, P]], channel_multiplier=1))
            link(pool.memset(neg_f[:], 0.0))
            link(pool.affine_select(out=neg_f[:], in_=neg_f[:], compare_op=ALU.is_ge, fill=NEG, base=-1,
                                    pattern=[[1, P]], channel_multiplier=-1))
            link(pool.memset(neg_s[:], 0.0))
            link(pool.affine_select(out=neg_s[:], in_=neg_s[:], compare_op=ALU.is_ge, fill=NEG, base=-1,
                                    pattern=[[1, SMP]], channel_multiplier=-1))
            v = neg_s[:].rearrange("p (s n) -> p s n", n=NEW)
            pool.affine_select(out=v, in_=v, compare_op=ALU.is_ge, fill=NEG, base=0,
                               pattern=[[-NEW, NSEQ], [0, NEW]], channel_multiplier=1).then_inc(pool_const, 1)
            with pool.Fori(0, U_END // 4) as i:
                for s in range(2):
                    pool.wait_ge(hi_done, 2 * i + s + 1)
                    pool.tensor_tensor(wlo[s][:], wraw[s][:], whi[s][:].bitcast(F32), ALU.subtract).then_inc(lo_done, 1)

        @block.scalar
        def _(act):
            act.preload_act_table_set("natural_log_exp_and_others")
            def wsplit(s, Pn, n_use, first=False):
                act.wait_ge(raw_landed[s], 32 * n_use)
                if not first:
                    act.wait_ge(unit_done, 2 * Pn - 2)
                act.activation(whi[s][:], wraw[s][:], ACT.Copy).then_inc(hi_done, 1)

            def wsplit_loop(Pb, n):
                with act.Fori(0, n) as i:
                    for s in range(2):
                        wsplit(s, Pb + 2 * i + s, Pb // 2 + 1 + i)

            act.dma_start(vec_rows[0:16, :], lb_logits.rearrange("a (m p) -> (a m) p", p=P)).then_inc(vec_landed, 16)
            for r, v in ((GON, g_onorm_a), (GMIX0, g_mix), (GMLP0, g_mlp)):
                n = v.shape[0] * NB
                act.dma_start(vec_rows[r:r + n, :], v.rearrange("a (m p) -> (a m) p", p=P)).then_inc(vec_landed, 16)
            for r, v in ((GKV, g_kv), (GFIN, g_final)):
                act.dma_start(vec_rows[r:r + NB, :], v.rearrange("(m p) -> m p", p=P)).then_inc(vec_landed, 16)
            act.dma_start(bias_row[:], sb_bias).then_inc(bias_landed, 16)
            act.dma_start(x_rows[:], x_prompt.rearrange("a (c p) d -> p (a c) d", p=P)).then_inc(x_landed, 16)
            act.dma_start(xs_rows[:], x_sample.rearrange("s n d -> (s n) d")).then_inc(x_landed, 16)
            act.dma_start(S0[:], state_hgrn[0, :, 0].rearrange("s k v -> k s v")).then_inc(s0_landed, 16)
            for s in range(2):
                wsplit(s, s, 1, first=True)
            act.wait_ge(pool_const, 1)
            act.activation(ones_r[:], ones[:], ACT.Copy).then_inc(act_const, 1)
            act.activation(ident_r[:], ident[:], ACT.Copy).then_inc(act_const, 1)
            act.wait_ge(lbs, 3)
            act.activation(small[:, 2 * NB:4 * NB], small[:, 0:2 * NB], ACT.Exp).then_inc(lbs_act, 1)
            for m in range(NB):
                act.wait_ge(xT_full, m + 1)
                act.activation(hT[:, m, 0:SEQ], pL[:, m % 2, :], ACT.Copy).then_inc(xT_read, 1)

            def squares(ready, m0=0, m1=NB):
                for m in range(m0, m1):
                    ready(m)
                    act.activation(nrm[:, m, :], hT[:, m, :], ACT.Square).then_inc(n_sq, 1)

            def norm_rstd(call):
                act.wait_ge(n_sum, call + 1)
                act.activation(rstd[:].rearrange(tok2, a=2), pL[:, :, 0:HALF], ACT.Ln, scale=1.0 / DM,
                               bias=eps_t[:, 0:1]).then_inc(n_rs, 1)
                act.wait_ge(n_rs, 2 * call + 1)
                act.activation(rstd[:], rstd[:], ACT.Exp, scale=-0.5).then_inc(n_rs, 1)

            def norm_hi(app, dst):
                for m in range(NB):
                    act.wait_ge(n_xf, NB * app + m + 1)
                    act.activation(dst[:, m, :], nrm[:, m, :], ACT.Copy).then_inc(n_hi, 1)

            def x_block(m):
                act.wait_ge(xT_read, NB)
                act.wait_ge(dve_const, 4)

            def split_and_norm(P0, n_use, ready, call, app):
                squares(ready, 0, 6)
                wsplit(0, P0, n_use)
                squares(ready, 6, NB)
                norm_rstd(call)
                norm_hi(app, xa_hi)
                wsplit(1, P0 + 1, n_use)

            squares(x_block)
            norm_rstd(0)
            norm_hi(0, xa_hi)
            act.wait_ge(pool_const, 3)
            act.activation(tri_r[:], tri_f[:], ACT.Copy).then_inc(tri_done, 1)
            act.activation(neg_r[:], neg_f[:], ACT.Copy).then_inc(tri_done, 1)

            def log_chain(src, dst, c, want):
                act.wait_ge(*want)
                act.wait_ge(c.sem, c.inc(act.activation(dst[:], src[:], ACT.Exp, scale=-1.0)))
                act.wait_ge(c.sem, c.inc(act.activation(dst[:], dst[:], ACT.Ln, bias=1.0)))

            def head_fz_q(h):
                c = Count(fz_act, 0, h, 5)
                cq = Count(q_act, 0, h, 3)
                log_chain(cl0, t1, c, (acc_free, 4 * h + 3))
                c.inc(act.activation(fg[:], t1[:], ACT.Exp, scale=-1.0))
                log_chain(qq, tq, cq, (acc_free, 4 * h + 4))
                cq.inc(act.activation(tq[:], tq[:], ACT.Exp, scale=-1.0))
                cq.end()
                act.wait_ge(fz_dve, 4 * h + 1)
                c.inc(act.activation(t2[:], t2[:], ACT.Exp, scale=-1.0))
                act.wait_ge(fz_dve, 4 * h + 2)
                c.inc(act.activation(fg[:], fg[:], ACT.Ln))
                c.end()

            def head_og(h):
                c = Count(og_act, 0, h, 3)
                log_chain(cl0, tq, c, (acc_free, 4 * h + 6))
                c.inc(act.activation(tq[:], tq[:], ACT.Exp, scale=-1.0))
                c.end()

            def head_prep(h):
                act.wait_ge(fz_dve, 4 * h + 4)
                act.activation(eG[:], G[:], ACT.Exp).then_inc(prep_act, 1)
                act.wait_ge(prep_dve, 4 * h + 1)
                act.activation(ek[:], ek[:], ACT.Exp).then_inc(prep_act, 1)
                for n in range(len(LEVELS)):
                    act.wait_ge(lev_D, len(LEVELS) * h + n + 1)
                    act.activation(D[n % 2][:, 0:TW[n]], D[n % 2][:, 0:TW[n]], ACT.Exp).then_inc(lev_E, 1)

            def head_finish(h):
                act.wait_ge(o_full, h + 1)
                act.activation(t1[:, 0:SEQ], pO[:], ACT.Square).then_inc(o_sq, 1)
                act.wait_ge(M_full, 4 * h + 3)
                act.activation(t1[:, SEQ:T], pM[:, 0:SMP], ACT.Square).then_inc(o_sq, 1)
                act.wait_ge(L_full, 14 * h + 14)
                act.wait_ge(L_free, 14 * h + 13)
                act.activation(rstd[:, 0:SEQ], pL[:, 1, :], ACT.Ln, scale=1.0 / P, bias=eps_t[:, 0:1]).then_inc(L_free, 1)
                act.wait_ge(M_full, 4 * h + 4)
                act.activation(rstd[:, SEQ:T], pM[:, SMP:2 * SMP], ACT.Ln, scale=1.0 / P,
                               bias=eps_t[:, 0:1]).then_inc(o_rs, 1)
                act.wait_ge(L_free, 14 * h + 14)
                act.wait_ge(o_rs, 2 * h + 1)
                act.activation(rstd[:], rstd[:], ACT.Exp, scale=-0.5).then_inc(o_rs, 1)

            def states_out(h):
                act.wait_ge(o_out, h + 1)
                act.dma_start(st_prompt[0, 0, bass.ds(h, 1)].rearrange("a k v -> k (a v)"), S[:, NCH - 1, :]
                              ).then_inc(state_stored, 16)
                act.dma_start(st_sample[0][:, bass.ds(h, 1)].rearrange("s a k v -> k (s a) v"), Sn[:]
                              ).then_inc(state_stored, 16)

            def head_units(h, lag):
                head_fz_q(h)
                wsplit(0, 2 * h + 2, h + 2)
                if lag is not None:
                    head_finish(lag)
                    act.wait_ge(o_out, h)
                head_prep(h)
                if lag is not None:
                    states_out(lag)
                    act.dma_start(S0[:], state_hgrn[0][:, bass.ds(h, 1)].rearrange("s a k v -> k (s a) v")
                                  ).then_inc(s0_landed, 16)
                head_og(h)
                wsplit(1, 2 * h + 3, h + 2)

            head_units(0, None)
            with act.Fori(1, NB) as h:
                head_units(h, h - 1)
            head_finish(NB - 1)
            states_out(NB - 1)
            for m in range(NB):
                act.activation(xa_hi[:, m, :], hgrn_o[:, m, :], ACT.Copy).then_inc(ho_hi, 1)
            wsplit_loop(U_OUT // 2 + 2, 1)

            def h_block(U):
                return lambda m: act.wait_ge(acc_free, U + m + 3)

            def mlp(Ub, Hb, norm_call, app):
                split_and_norm(Ub // 2, Ub // 4 + 1, h_block(Ub - NB), norm_call, app)

                def chunk(c, n_split):
                    with act.Fori(0, 2) as i:
                        for s in range(2):
                            for a in range(2):
                                U = Ub + 16 * c + 4 * i + 2 * s + a
                                n = Hb + NB * c + 4 * i + 2 * s + a
                                act.wait_ge(unit_done, U + 1)
                                act.wait_ge(acc_free, U + 2)
                                act.activation(relu_t[a][:].rearrange(tok2, a=2), acc[a][:, :, 0:HALF], ACT.Relu
                                               ).then_inc(acc_free, 1)
                                act.wait_ge(sqr_done, n + 1)
                                act.activation(xb_hi[:, bass.ds(4 * i + 2 * s + a, 1), :].rearrange("p a t -> p (a t)"),
                                               sqr_t[a][:], ACT.Copy).then_inc(hid_hi, 1)
                            wsplit(s, Ub // 2 + 8 * c + 2 * i + s + 2, Ub // 4 + 4 * c + i + 2)
                    with act.Fori(0, n_split) as i:
                        for s in range(2):
                            wsplit(s, Ub // 2 + 8 * c + 4 + 2 * i + s + 2, Ub // 4 + 4 * c + i + 4)

                with act.Fori(0, FCH - 1) as c:
                    chunk(c, 2)
                chunk(FCH - 1, 1)

            mlp(U_MLP0, 0, n_norm["mlp0"], n_app["mlp0"])
            split_and_norm(U_Q // 2, U_Q // 4 + 1, h_block(U_Q - NB), n_norm["mix1"], n_app["q"])
            norm_hi(n_app["kv"], xb_hi)
            wsplit_loop(U_Q // 2 + 2, 2)

            def soft3(src, dst, n, sm):
                act.activation(dst, src, ACT.Abs).then_inc(sm, 1)
                act.wait_ge(sm, n + 1)
                act.activation(dst, dst, ACT.Exp, scale=-1.0).then_inc(sm, 1)
                act.wait_ge(sm, n + 2)
                act.activation(dst, dst, ACT.Ln, bias=1.0).then_inc(sm, 1)

            def pair(j, par, nxt):
                act.wait_ge(acc_free, U_KV + 2 * j + 3)
                act.activation(khi[:], kf[:], ACT.Copy).then_inc(k_hi, 1)
                act.activation(qhi[:], qT[:, bass.ds(j, 1), 0:SEQ].rearrange("p a t -> p (a t)"), ACT.Copy).then_inc(q_hi, 1)
                act.wait_ge(B_free, 8 * j + 2 + 2)
                act.dma_start(k_out[:, :, bass.ds(j * P, P)], kr[:]).then_inc(kv_stored, 16)
                act.dma_start(v_out[:, :, bass.ds(j * P, P)], vr[:]).then_inc(kv_stored, 16)
                for n in range(7):
                    N = 6 * j + n
                    if n >= 1:
                        hh, g = divmod(n - 1, 3)
                        cols = slice(GCOL[g], GCOL[g] + GW[g])
                        act.wait_ge(sp_done, N)
                        act.activation(uh[hh][:, cols], tl[(n - 1) % 2][:, 0:GW[g]], ACT.Copy).then_inc(u_hi, 1)
                    if n < 6:
                        g = n % 3
                        act.wait_ge(B_free, 8 * j + n + 5)
                        soft3(zb[n % 2][:, 0:GW[g]], tl[n % 2][:, 0:GW[g]], 3 * N, soft)
                    if n >= 1:
                        hh, g = divmod(n - 1, 3)
                        if (hh, g) == (1, 0):
                            act.wait_ge(AV_full, 2 * j + 1)
                        act.wait_ge(la_done, N + 1)
                        act.activation(Am[:, GCOL[g]:GCOL[g] + GW[g]], zb[(n - 1) % 2][:, 0:GW[g]], ACT.Exp
                                       ).then_inc(a_done, 1)

            def pair_split(par, i, j):
                wsplit(1 - par, U_KV // 2 + j + 3, U_KV // 4 + i + 2 + par)

            wsplit(0, U_KV // 2 + 2, U_KV // 4 + 2)
            with act.Fori(0, NPAIR // 2 - 1) as i:
                for par in range(2):
                    pair(2 * i + par, par, True)
                    pair_split(par, i, 2 * i + par)
            pair(NPAIR - 2, 0, True)
            pair_split(0, NPAIR // 2 - 1, NPAIR - 2)
            pair(NPAIR - 1, 1, False)

            act.wait_ge(new_dve, 2)
            soft3(zbN[:], tlN[:], 0, new_act)
            act.wait_ge(new_dve, 3)
            act.activation(uhN[:], tlN[:], ACT.Copy).then_inc(new_act, 1)
            act.dma_start(k_sample.rearrange("s n h d -> (s n) (h d)"), kvn[:, 0].rearrange("p j f -> p (j f)")
                          ).then_inc(kv_stored, 16)
            act.dma_start(v_sample.rearrange("s n h d -> (s n) (h d)"), kvn[:, 1].rearrange("p j f -> p (j f)")
                          ).then_inc(kv_stored, 16)
            act.wait_ge(new_dve, 5)
            act.wait_ge(kv_stored, 32 * NPAIR + 32)
            act.activation(AN[:], zbN[:], ACT.Exp).then_inc(new_act, 1)

            def t_copy(s, f):
                act.wait_ge(T_full, 8 * s + f + 1)
                act.activation(KT[:, 4 * (f % 2):4 * (f % 2) + 4, f // 2, :],
                               T_bank(f).rearrange("p (j k) -> p j k", k=P), ACT.Copy).then_inc(Ta_free, 1)

            def seq(s, nxt):
                act.wait_ge(zS_dve, 5 * s + 1)
                soft3(zbS[:], tlS[:], 4 * s, zS_act)
                if nxt:
                    t_copy(s + 1, 0)
                    t_copy(s + 1, 2)
                act.wait_ge(zS_dve, 5 * s + 4)
                act.activation(AS[:], zbS[:], ACT.Exp).then_inc(zS_act, 1)
                if nxt:
                    t_copy(s + 1, 4)
                    t_copy(s + 1, 6)

            for f in (0, 2, 4, 6):
                t_copy(0, f)
            with act.Fori(0, NSEQ - 1) as s:
                seq(s, True)
            seq(NSEQ - 1, False)
            for m in range(NB):
                act.wait_ge(fin_free, 2 * NSEQ)
                act.activation(xb_hi[:, m, :], attn_o[:, m, :], ACT.Copy).then_inc(ao_hi, 1)
            wsplit_loop(U_OB // 2 + 2, 1)
            mlp(U_MLP1, FCH * NB, n_norm["mlp1"], n_app["mlp1"])
            squares(h_block(U_END - NB))
            norm_rstd(n_norm["final"])
            for n in range(SEQ // P + 1):
                w = P if n < SEQ // P else SMP
                act.wait_ge(y_full, 2 * n + 1)
                if n:
                    act.wait_ge(y_read, 2 * n)
                if n >= 2:
                    act.wait_ge(y_stored[n % 2], 16 * (n // 2))
                act.activation(yrow[n % 2][0:w, 0:512], pL[0:w, 0, :], ACT.Copy).then_inc(y_read, 1)

        @block.vector
        def _(dve):
            def lo_part(dst, hi, full, sem_hi, count):
                dve.wait_ge(sem_hi, count)
                dve.tensor_tensor(dst, full, hi.bitcast(F32), ALU.subtract).then_inc(x_ready, 1)

            for n, q in enumerate((B_free, B_free, a_done, a_done, AV_free, la_done)):
                dve.memset(start_mark[0:1, n:n + 1], 0.0).then_inc(q, 1)
            dve.memset(eps_t[:], EPS).then_inc(acc_free, 1)
            dve.memset(Amat[:], 0.0).then_inc(acc_free, 1)
            dve.memset(As[:], 0.0).then_inc(dve_const, 1)
            dve.wait_ge(vec_T, 1)
            dve.tensor_copy(gT[:], pO[:, 0:72]).then_inc(dve_const, 1)
            dve.tensor_copy(bias_h[:], pO[:, 72:72 + H_B]).then_inc(dve_const, 1)
            dve.wait_ge(dve_const, 2)
            dve.tensor_tensor(small[:, 2 * NB:3 * NB], gT[:, LB0:LB0 + NB], gT[:, LB1:LB1 + NB], ALU.max).then_inc(lbs, 1)
            dve.wait_ge(lbs, 1)
            dve.tensor_tensor(small[:, 0:NB], gT[:, LB0:LB0 + NB], small[:, 2 * NB:3 * NB], ALU.subtract).then_inc(lbs, 1)
            dve.tensor_tensor(small[:, NB:2 * NB], gT[:, LB1:LB1 + NB], small[:, 2 * NB:3 * NB], ALU.subtract).then_inc(lbs, 1)
            dve.wait_ge(lbs_act, 1)
            dve.tensor_tensor(small[:, 0:NB], small[:, 2 * NB:3 * NB], small[:, 3 * NB:4 * NB], ALU.add).then_inc(lbs, 1)
            dve.wait_ge(lbs, 4)
            dve.reciprocal(small[:, NB:2 * NB], small[:, 0:NB]).then_inc(lbs, 1)
            dve.wait_ge(lbs, 5)
            dve.tensor_tensor(small[:, 2 * NB:3 * NB], small[:, 2 * NB:3 * NB], small[:, NB:2 * NB], ALU.mult).then_inc(lbs, 1)
            dve.tensor_tensor(omlb[:], small[:, 3 * NB:4 * NB], small[:, NB:2 * NB], ALU.mult).then_inc(lbs, 1)
            dve.wait_ge(lbs, 6)
            dve.tensor_scalar(lb[:], small[:, 2 * NB:3 * NB], 2.0 ** -60, None, ALU.max).then_inc(lbs, 1)
            dve.wait_ge(xT_full, NB + 1)
            dve.tensor_copy(hT[:, :, SEQ:T], pM[:].rearrange("p (m t) -> p m t", t=SMP)).then_inc(dve_const, 1)

            def norm_apply(call, app, g, hi, lo):
                dve.wait_ge(n_rs, 2 * call + 2)
                for m in range(NB + 2):
                    if m < NB:
                        dve.scalar_tensor_tensor(out=nrm[:, m, :], in0=hT[:, m, :], scalar=gT[:, g + m:g + m + 1],
                                                 in1=rstd[:], op0=ALU.mult, op1=ALU.mult).then_inc(n_xf, 1)
                    if m >= 2:
                        dve.wait_ge(n_xf, NB * app + m - 1)
                        lo_part(lo[:, m - 2, :], hi[:, m - 2, :], nrm[:, m - 2, :], n_hi, NB * app + m - 1)

            def add_square(call, m):
                dve.wait_ge(n_sq, NB * call + m + 1)
                if m > 1:
                    dve.wait_ge(n_tot, (NB - 1) * call + m - 1)
                dve.tensor_tensor(nrm[:, 0, :], nrm[:, 0, :], nrm[:, m, :], ALU.add).then_inc(n_tot, 1)

            for m in range(1, NB):
                add_square(0, m)
            norm_apply(n_norm["mix0"], n_app["mix0"], GMIX0, xa_hi, xa_lo)

            def accv(a):
                return acc[a][:, :, 0:HALF]

            def t2v(t):
                return t[:].rearrange(tok2, a=2)

            def head_gates(h):
                if not isinstance(h, int) or h:
                    dve.wait_ge(og_dve, h)
                dve.wait_ge(unit_done, 4 * h + 1)
                dve.tensor_scalar(t2v(cl0), accv(0), CLAMP, None, ALU.max).then_inc(acc_free, 1)
                dve.wait_ge(unit_done, 4 * h + 2)
                dve.tensor_scalar(t2v(qq), accv(1), CLAMP, None, ALU.max).then_inc(acc_free, 1)

            def head_fz_q(h, step):
                if step == 0:
                    dve.wait_ge(fz_act, 5 * h + 2)
                    dve.wait_ge(acc_free, 4 * h + 3)
                    dve.tensor_tensor(t2[:], cl0[:], t1[:], ALU.add).then_inc(fz_dve, 1)
                if step == 1:
                    dve.wait_ge(fz_act, 5 * h + 3)
                    dve.tensor_scalar(fg[:], fg[:], omlb[:, bass.ds(h, 1)], lb[:, bass.ds(h, 1)], ALU.mult, ALU.add
                                      ).then_inc(fz_dve, 1)
                if step == 2:
                    dve.wait_ge(q_act, 3 * h + 3)
                    dve.wait_ge(acc_free, 4 * h + 4)
                    dve.tensor_tensor(qq[:], qq[:], tq[:], ALU.mult).then_inc(q_dve, 1)
                if step == 3:
                    dve.wait_ge(fz_act, 5 * h + 4)
                    dve.tensor_scalar(kk[:], t2[:], omlb[:, bass.ds(h, 1)], None, ALU.mult).then_inc(fz_dve, 1)
                if step == 4:
                    dve.wait_ge(fz_act, 5 * h + 5)
                    dve.tensor_tensor_scan(G[:], scan_keep[:], fg[:], 0.0, ALU.mult, ALU.add).then_inc(fz_dve, 1)

            def head_v(h):
                dve.wait_ge(unit_done, 4 * h + 3)
                dve.tensor_copy(t2v(vT), accv(0)).then_inc(acc_free, 1)

            def head_og(h):
                dve.wait_ge(unit_done, 4 * h + 4)
                dve.tensor_scalar(t2v(cl0), accv(1), CLAMP, None, ALU.max).then_inc(acc_free, 1)
                dve.wait_ge(og_act, 3 * h + 3)
                dve.wait_ge(acc_free, 4 * h + 6)
                dve.scalar_tensor_tensor(out=sgg[:], in0=cl0[:], scalar=gT[:, bass.ds(GON + h, 1)], in1=tq[:],
                                         op0=ALU.mult, op1=ALU.mult).then_inc(og_dve, 1)

            def head_prep(h):
                c = Count(prep_dve, 0, h, 4)
                dve.wait_ge(fz_dve, 4 * h + 4)
                dve.wait_ge(q_dve, h + 1)
                Gp = G[:, 0:SEQ].rearrange("p (c t) -> p c t", t=CH)
                Gs = G[:, SEQ:T].rearrange("p (c t) -> p c t", t=NEW)
                ekp = ek[:, 0:SEQ].rearrange("p (c t) -> p c t", t=CH)
                eks = ek[:, SEQ:T].rearrange("p (c t) -> p c t", t=NEW)
                dve.tensor_tensor(ekp, Gp[:, :, CH - 1:CH].to_broadcast([P, NCH, CH]), Gp, ALU.subtract)
                c.inc(dve.tensor_tensor(eks, Gs[:, :, NEW - 1:NEW].to_broadcast([P, NSEQ, NEW]), Gs, ALU.subtract))
                n_lv = len(LEVELS)

                def diffs(n):
                    m, w = LEVELS[n], TW[n]
                    if n >= 2:
                        dve.wait_ge(lev_X, 2 * n_lv * h + 2 * (n - 2) + 2)
                    Gv = G[:, 0:w].rearrange("p (b j) -> p b j", j=2 * m)
                    Dv = D[n % 2][:, 0:w].rearrange("p (b j) -> p b j", j=2 * m)
                    mid = Gv[:, :, m - 1:m].to_broadcast([P, w // (2 * m), m])
                    dve.tensor_tensor(Dv[:, :, 0:m], mid, Gv[:, :, 0:m], ALU.subtract)
                    dve.tensor_tensor(Dv[:, :, m:2 * m], Gv[:, :, m:2 * m], mid, ALU.subtract).then_inc(lev_D, 1)

                def factors(n):
                    m, w = LEVELS[n], TW[n]
                    dve.wait_ge(lev_E, n_lv * h + n + 1)
                    Ev = D[n % 2][:, 0:w].rearrange("p (b j) -> p b j", j=2 * m)
                    Xv = X[n][:, 0:w].rearrange("p (b j) -> p b j", j=2 * m)
                    kv = kk[:, 0:w].rearrange("p (b j) -> p b j", j=2 * m)
                    qv = qq[:, 0:w].rearrange("p (b j) -> p b j", j=2 * m)
                    dve.tensor_tensor(Xv[:, :, 0:m], Ev[:, :, 0:m], kv[:, :, 0:m], ALU.mult).then_inc(lev_X, 1)
                    dve.tensor_tensor(Xv[:, :, m:2 * m], Ev[:, :, m:2 * m], qv[:, :, m:2 * m], ALU.mult).then_inc(lev_X, 1)

                diffs(0)
                c.inc(dve.tensor_tensor(dg[:], qq[:], kk[:], ALU.mult))
                dve.wait_ge(prep_act, 2 * h + 1)
                c.inc(dve.tensor_tensor(qe[:], qq[:], eG[:], ALU.mult))
                dve.wait_ge(prep_act, 2 * h + 2)
                c.inc(dve.tensor_tensor(kh[:], kk[:], ek[:], ALU.mult))
                c.end()
                for n in range(n_lv):
                    if n + 1 < n_lv:
                        diffs(n + 1)
                    factors(n)
                    if n == 2:
                        head_v(h)

            def head_products(h, first, nxt):
                if nxt is not None:
                    head_gates(nxt)
                Lb, Mb = 14 * h, 4 * h
                for n in range(2):
                    dve.wait_ge(L_full, Lb + n + 1)
                    dve.tensor_copy(VK[:, n, 0:NCH, :], pL[:, n, :].rearrange("p (c d) -> p c d", d=P)).then_inc(L_free, 1)
                dve.wait_ge(M_full, Mb + 1)
                dve.tensor_copy(VK[0:SMP, :, NCH, :], pM[0:SMP, 0:2 * P].rearrange("p (n d) -> p n d", d=P)
                                ).then_inc(M_free, 1)
                for n in range(len(LEVELS) + 1):
                    mk = (masks[:, n:n + 1, :] if n < len(LEVELS) else ident[:].rearrange("p (a t) -> p a t", a=1))
                    dve.wait_ge(L_free, Lb + n + 2)
                    dve.wait_ge(L_full, Lb + n + 3)
                    dve.memset(wait_mark[0:1, n:n + 1], 0.0)
                    dve.copy_predicated(Amat[:], mk.to_broadcast([P, NCH, P]).bitcast(U32),
                                        pL[:, n % 2, :].rearrange("p (c t) -> p c t", t=P)).then_inc(L_free, 1)
                    if nxt is not None and n < 5:
                        head_fz_q(nxt, n)
                dve.wait_ge(M_full, Mb + 2)
                dve.memset(wait_mark[0:1, 15:16], 0.0)
                for n in range(SMP_LEVELS + 1):
                    mk = masks[0:SMP, len(LEVELS) - SMP_LEVELS + n, 0:SMP] if n < SMP_LEVELS else ident[0:SMP, 0:SMP]
                    if n:
                        dve.wait_ge(as_chain, SMP_LEVELS * h + n)
                        dve.memset(wait_mark[0:1, 10 + n:11 + n], 0.0)
                    dve.copy_predicated(As[:], mk.bitcast(U32), pM[0:SMP, 2 * P + n * SMP:2 * P + (n + 1) * SMP]
                                        ).then_inc(as_chain if n < SMP_LEVELS else M_free, 1)
                dve.wait_ge(M_free, 3 * h + 1)
                dve.tensor_tensor(Vblk[:], VK[0:SMP, 0, NCH:NCH + 1, :].to_broadcast([SMP, NSEQ, P]),
                                  seqmask[:].rearrange("p (s a) -> p s a", a=1).to_broadcast([SMP, NSEQ, P]), ALU.mult
                                  ).then_inc(vblk_ready, 1)
                dve.wait_ge(L_full, Lb + 11)
                if not first:
                    dve.wait_ge(state_stored, 32 * h)
                for n in range(NCH):
                    kv = pL[:, 0, n * P:(n + 1) * P]
                    if n == 0:
                        dve.tensor_copy(S[:, 0, :], kv).then_inc(s_chain, 1)
                        continue
                    dve.wait_ge(s_chain, 3 * h + n)
                    ins = dve.scalar_tensor_tensor(out=S[:, n, :], in0=S[:, n - 1, :],
                                                   scalar=eG[:, n * CH + CH - 1:n * CH + CH], in1=kv,
                                                   op0=ALU.mult, op1=ALU.add)
                    ins.then_inc(s_chain if n < NCH - 1 else L_free, 1)
                dve.wait_ge(s0_landed, 16 * h + 16)
                dve.tensor_tensor(Sn[:], S0[:], eG[:, SEQ + NEW - 1:T:NEW].rearrange("p (s a) -> p s a", a=1)
                                  .to_broadcast([P, NSEQ, P]), ALU.mult).then_inc(sn_scaled, 1)
                dve.wait_ge(sn_scaled, h + 1)
                for n in range(2):
                    dve.wait_ge(L_full, Lb + 12 + n)
                    dve.tensor_tensor(Sn[:, 4 * n:4 * n + 4, :], Sn[:, 4 * n:4 * n + 4, :],
                                      pL[:, (n + 1) % 2, :].rearrange("p (s v) -> p s v", v=P), ALU.add).then_inc(L_free, 1)
                dve.wait_ge(o_rs, 2 * h + 2)
                dve.tensor_tensor(t2[:, 0:SEQ], pO[:], rstd[:, 0:SEQ], ALU.mult).then_inc(o_norm, 1)
                dve.tensor_tensor(t2[:, SEQ:T], pM[:, 0:SMP], rstd[:, SEQ:T], ALU.mult).then_inc(M_free, 1)
                dve.wait_ge(o_norm, h + 1)
                dve.wait_ge(M_free, 3 * h + 3)
                dve.wait_ge(og_dve, h + 1)
                dve.tensor_tensor(hgrn_o[:, bass.ds(h, 1), :].rearrange("p a t -> p (a t)"), t2[:], sgg[:], ALU.mult
                                  ).then_inc(o_out, 1)

            dve.wait_ge(pool_const, 2)
            head_gates(0)
            for n in range(5):
                head_fz_q(0, n)
            head_prep(0)
            head_og(0)
            head_products(0, True, 1)
            head_prep(1)
            head_og(1)
            with dve.Fori(2, NB) as h:
                head_products(h - 1, False, h)
                head_prep(h)
                head_og(h)
            head_products(NB - 1, False, None)
            for m in range(NB):
                lo_part(xa_lo[:, m, :], xa_hi[:, m, :], hgrn_o[:, m, :], ho_hi, m + 1)

            def add_to_h(Ub):
                with dve.Fori(0, 4) as i:
                    for a in range(2):
                        hv = hT[:, bass.ds(2 * i + a, 1), :].rearrange("p o (a b) -> p (o a) b", a=2)
                        dve.wait_ge(unit_done, Ub + 2 * i + a + 1)
                        dve.tensor_tensor(hv, hv, accv(a), ALU.add).then_inc(acc_free, 1)

            def add_to_h_last(Ub, call):
                for m in range(NB):
                    hv = hT[:, m, :].rearrange(tok2, a=2)
                    dve.wait_ge(unit_done, Ub + m + 1)
                    dve.tensor_tensor(hv, hv, accv(m % 2), ALU.add).then_inc(acc_free, 1)
                    if m > 1:
                        add_square(call, m - 1)
                add_square(call, NB - 1)

            add_to_h_last(U_OUT, n_norm["mlp0"])

            def mlp(Ub, Hb, hid_hi_t, hid_lo_t, next_norm):
                def hidden(c):
                    with dve.Fori(0, 4) as i:
                        for a in range(2):
                            n = Hb + NB * c + 2 * i + a
                            hb = bass.ds(2 * i + a, 1)
                            dve.wait_ge(acc_free, Ub + 16 * c + 2 * i + a + 3)
                            dve.tensor_tensor(sqr_t[a][:], relu_t[a][:], relu_t[a][:], ALU.mult).then_inc(sqr_done, 1)
                            dve.wait_ge(sqr_done, n + 1)
                            lo_part(hid_lo_t[:, hb, :].rearrange("p a t -> p (a t)"),
                                    hid_hi_t[:, hb, :].rearrange("p a t -> p (a t)"), sqr_t[a][:], hid_hi, n + 1)

                with dve.Fori(0, FCH - 1) as c:
                    hidden(c)
                    add_to_h(Ub + 16 * c + 8)
                hidden(FCH - 1)
                add_to_h_last(Ub + 16 * FCH - 8, next_norm)

            norm_apply(n_norm["mlp0"], n_app["mlp0"], GMLP0, xa_hi, xa_lo)
            dve.wait_ge(state_stored, 32 * NB)
            mlp(U_MLP0, 0, xb_hi, xb_lo, n_norm["mix1"])
            norm_apply(n_norm["mix1"], n_app["q"], GMIX1, xa_hi, xa_lo)
            dve.wait_ge(n_hi, NB * n_app["kv"])
            dve.wait_ge(x_ready, X_KV)
            norm_apply(n_norm["mix1"], n_app["kv"], GKV, xb_hi, xb_lo)
            with dve.Fori(0, 4) as i:
                for a in range(2):
                    dve.wait_ge(unit_done, U_Q + 2 * i + a + 1)
                    dve.tensor_copy(qT[:, bass.ds(2 * i + a, 1), :].rearrange("p o (a b) -> p (o a) b", a=2), accv(a)
                                    ).then_inc(acc_free, 1)

            def kv_copy(U, a):
                dve.wait_ge(unit_done, U + a + 1)
                dve.tensor_copy(t2v((kf, vf)[a]), accv(a)).then_inc(acc_free, 1)

            def pair(j, nxt):
                U = U_KV + 2 * j
                dve.wait_ge(acc_free, U + 3)
                dve.tensor_copy(kTs[:, bass.ds(j, 1), :].rearrange("p a t -> p (a t)"), kf[:, SEQ:T]).then_inc(kts_done, 1)
                dve.wait_ge(k_hi, j + 1)
                dve.tensor_tensor(klo[:], kf[:], khi[:].bitcast(F32), ALU.subtract).then_inc(kq_lo, 1)
                dve.wait_ge(q_hi, j + 1)
                dve.tensor_tensor(qlo[:], qT[:, bass.ds(j, 1), 0:SEQ].rearrange("p a t -> p (a t)"),
                                  qhi[:].bitcast(F32), ALU.subtract).then_inc(kq_lo, 1)
                if not isinstance(j, int) or j:
                    dve.wait_ge(kv_stored, 32 * j)
                for n, t in enumerate((kr, vr)):
                    dve.wait_ge(B_full, 8 * j + n + 1)
                    dve.tensor_copy(t[:], pL[:, n, :].rearrange("p (c f) -> p c f", f=P)).then_inc(B_free, 1)
                dve.wait_ge(R_full, 7 * j + 1)
                dve.tensor_copy(kvn[:, :, bass.ds(j, 1), :].rearrange("p n a f -> p n (a f)"),
                                pM[0:SMP, 0:2 * P].rearrange("p (n f) -> p n f", f=P)).then_inc(R_free, 1)
                for n in range(7):
                    N = 6 * j + n
                    if n < 6:
                        hh, g = divmod(n, 3)
                        dve.wait_ge(a_done, N + 1)
                        dve.wait_ge(B_full, 8 * j + n + 3)
                        dve.tensor_scalar(zb[n % 2][:, 0:GW[g]], pL[:, n % 2, 0:GW[g]], SCALE,
                                          bias_h[:, bass.ds(2 * j + hh, 1)], ALU.mult, ALU.add).then_inc(B_free, 1)
                    if n >= 1:
                        hh, g = divmod(n - 1, 3)
                        cols = slice(GCOL[g], GCOL[g] + GW[g])
                        dve.wait_ge(u_hi, N)
                        dve.tensor_tensor(ul[hh][:, cols], tl[(n - 1) % 2][:, 0:GW[g]],
                                          uh[hh][:, cols].bitcast(F32), ALU.subtract).then_inc(u_lo, 1)
                        zv = zb[(n - 1) % 2][:, 0:GW[g]]
                        dve.wait_ge(sp_done, N)
                        dve.wait_ge(R_full, 7 * j + n + 1)
                        dve.tensor_tensor(zv, zv, pM[:, 0:GW[g]], ALU.subtract).then_inc(la_done, 1)
                    if n < 6:
                        g = n % 3
                        dve.wait_ge(soft, 3 * N + 3)
                        dve.wait_ge(B_free, 8 * j + n + 5)
                        tv = tl[n % 2][:, 0:GW[g]]
                        dve.scalar_tensor_tensor(out=tv, in0=zb[n % 2][:, 0:GW[g]], scalar=0.0, in1=tv,
                                                 op0=ALU.max, op1=ALU.add).then_inc(sp_done, 1)
                    if nxt and n in (2, 5):
                        kv_copy(U + 2, (n - 2) // 3)
                    if n in (4, 6):
                        hh = n // 2 - 2
                        rows = slice(64 * hh, 64 * hh + 64)
                        dve.wait_ge(AV_full, 2 * j + hh + 1)
                        dve.tensor_copy(attn_o[rows, bass.ds(j, 1), 0:SEQ].rearrange("p a t -> p (a t)"), pO[rows, :]
                                        ).then_inc(AV_free, 1)

            kv_copy(U_KV, 0)
            kv_copy(U_KV, 1)
            pair(0, True)
            with dve.Fori(1, NPAIR - 1) as j:
                pair(j, True)
            pair(NPAIR - 1, False)

            dve.wait_ge(AV_free, 2 * NPAIR + 1)
            dve.wait_ge(kv_stored, 32 * NPAIR)
            dve.memset(QB0[:], 0.0).then_inc(qblk_done, 1)
            dve.memset(QB1[:], 0.0).then_inc(qblk_done, 1)
            dve.tensor_copy(qTs[:], qT[:, :, SEQ:T]).then_inc(qblk_done, 1)
            dve.tensor_tensor(bias_m[:], bias_h[:], row_head[:], ALU.mult).then_inc(new_chain, 1)
            dve.wait_ge(new_chain, 1)
            dve.tensor_reduce(row_bias[:], bias_m[:], mybir.AxisListType.X, ALU.add).then_inc(new_chain, 1)
            bcol = bias_h[:].rearrange("p (h a) -> p h a", a=1)
            dve.tensor_tensor(biasN[:], bcol[0:SMP].to_broadcast([SMP, H_B, SMP]),
                              neg_s[:].rearrange("p (a t) -> p a t", a=1).to_broadcast([SMP, H_B, SMP]), ALU.add
                              ).then_inc(new_chain, 1)
            dve.wait_ge(new_chain, 3)
            dve.wait_ge(new_full, 1)
            zN = pL[0:SMP].rearrange("p a b -> p (a b)")
            zbNf, tlNf = (t[:].rearrange("p h t -> p (h t)") for t in (zbN, tlN))
            for e in range(2):
                zb_e, bias_e = (t[:].rearrange("p (j e) t -> p j e t", e=2)[:, :, e, :] for t in (zbN, biasN))
                dve.scalar_tensor_tensor(out=zb_e, in0=pL[0:SMP, e, :].rearrange("p (j t) -> p j t", t=SMP),
                                         scalar=SCALE, in1=bias_e, op0=ALU.mult, op1=ALU.add).then_inc(new_dve, 1)
            dve.wait_ge(new_dve, 2)
            dve.wait_ge(new_act, 3)
            dve.scalar_tensor_tensor(out=tlNf, in0=zbNf, scalar=0.0, in1=tlNf, op0=ALU.max, op1=ALU.add).then_inc(new_dve, 1)
            dve.wait_ge(new_dve, 3)
            for s in range(NSEQ):
                dve.tensor_copy(tlNs[:, s, :].rearrange("p (h n) -> p h n", n=NEW), tlN[:, :, s * NEW:(s + 1) * NEW]
                                ).then_inc(new_chain, 1)
            dve.wait_ge(new_act, 4)
            dve.tensor_tensor(ulN[:], tlN[:], uhN[:].bitcast(F32), ALU.subtract).then_inc(new_dve, 1)
            dve.wait_ge(new_full, 2)
            dve.tensor_tensor(zbNf, zbNf, zN, ALU.subtract).then_inc(new_dve, 1)
            dve.tensor_copy(newR[:], pM[:, 0:NSEQ]).then_inc(new_chain, 1)
            dve.wait_ge(new_dve, 5)
            dve.wait_ge(new_act, 5)
            dve.memset(wait_mark[0:1, 0:1], 0.0).then_inc(qblk_done, 1)

            def queries(s, b):
                if isinstance(s, int) and s < 2:
                    dve.wait_ge(qblk_done, 3)
                for hh in range(2):
                    rows = slice(64 * hh, 64 * hh + 64)
                    dve.tensor_copy(QB[b][:].rearrange("p j c -> p (j c)").rearrange("p (j c) -> p j c", c=P + 2 * NEW)
                                    [rows, :, hh * NEW:(hh + 1) * NEW], qTs[rows, :, bass.ds(NEW * s, NEW)]
                                    ).then_inc(QB_ready, 1)
                dve.tensor_copy(ANs[b][:].rearrange("p (h n) -> p h n", n=NEW), AN[:, :, bass.ds(NEW * s, NEW)]
                                ).then_inc(ANs_ready, 1)

            queries(0, 0)

            def t_copy(s, f):
                dve.wait_ge(T_full, 8 * s + f + 1)
                dve.tensor_copy(KT[:, 4 * (f % 2):4 * (f % 2) + 4, f // 2, :],
                                T_bank(f).rearrange("p (j k) -> p j k", k=P)).then_inc(Td_free, 1)

            def finish(s):
                dve.wait_ge(fin_full, s + 1)
                for hh in range(2):
                    rows = slice(64 * hh, 64 * hh + 64)
                    dve.tensor_copy(attn_o[rows, :, bass.ds(SEQ + NEW * s, NEW)],
                                    pM[rows, 0:P].rearrange("p (j c) -> p j c", c=2 * NEW)[:, :, hh * NEW:(hh + 1) * NEW]
                                    ).then_inc(fin_free, 1)

            def seq(s, b, first, nxt):
                dve.wait_ge(zS_full, s + 1)
                dve.tensor_scalar(zbS[:], pM[:], SCALE, row_bias[:, 0:1], ALU.mult, ALU.add).then_inc(zS_dve, 1)
                if nxt:
                    t_copy(s + 1, 1)
                dve.wait_ge(zS_dve, 5 * s + 1)
                dve.wait_ge(zS_act, 4 * s + 3)
                dve.scalar_tensor_tensor(out=tlS[:], in0=zbS[:], scalar=0.0, in1=tlS[:], op0=ALU.max, op1=ALU.add
                                         ).then_inc(zS_dve, 1)
                if nxt:
                    t_copy(s + 1, 3)
                dve.wait_ge(zS_dve, 5 * s + 2)
                dve.tensor_tensor_scan(RS[:, ::-1], ones[:, 0:1].to_broadcast([P, 512]), tlS[:, ::-1],
                                       0.0, ALU.mult, ALU.add).then_inc(zS_dve, 1)
                dve.wait_ge(zS_dve, 5 * s + 3)
                dve.scalar_tensor_tensor(out=zbS[:], in0=zbS[:], scalar=newR[:, bass.ds(s, 1)], in1=RS[:],
                                         op0=ALU.subtract, op1=ALU.subtract).then_inc(zS_dve, 1)
                if nxt:
                    t_copy(s + 1, 5)
                dve.wait_ge(AT_full, s + 1)
                dve.tensor_copy(AT[:].rearrange("p g c -> p (g c)"), pO[:]).then_inc(zS_dve, 1)
                if not first:
                    finish(s - 1)
                if nxt:
                    t_copy(s + 1, 7)
                    queries(s + 1, 1 - b)
                dve.wait_ge(O_full, s + 1)
                dve.tensor_tensor(O_m[:], acc[1][:].rearrange("p a f -> p (a f)").rearrange("p (j f) -> p j f", f=P),
                                  row_pair[:].rearrange("p (j a) -> p j a", a=1).to_broadcast([P, NPAIR, P]), ALU.mult
                                  ).then_inc(O_dve, 1)
                dve.wait_ge(O_dve, 2 * s + 1)
                dve.tensor_reduce(Oc[:], O_m[:].rearrange("p j f -> p f j"), mybir.AxisListType.X, ALU.add
                                  ).then_inc(O_dve, 1)

            for f in (1, 3, 5, 7):
                t_copy(0, f)
            seq(0, 0, True, True)
            with dve.Fori(0, NSEQ // 2 - 1) as i:
                for n in range(2):
                    seq(2 * i + 1 + n, 1 - n, False, True)
            seq(NSEQ - 1, 1, False, False)
            finish(NSEQ - 1)
            dve.wait_ge(fin_free, 2 * NSEQ)
            for m in range(NB):
                lo_part(xb_lo[:, m, :], xb_hi[:, m, :], attn_o[:, m, :], ao_hi, m + 1)
            add_to_h_last(U_OB, n_norm["mlp1"])
            norm_apply(n_norm["mlp1"], n_app["mlp1"], GMLP1, xa_hi, xa_lo)
            mlp(U_MLP1, FCH * NB, xb_hi, xb_lo, n_norm["final"])
            dve.wait_ge(n_rs, 2 * n_norm["final"] + 2)
            for m in range(NB):
                dve.scalar_tensor_tensor(out=nrm[:, m, :], in0=hT[:, m, :], scalar=gT[:, GFIN + m:GFIN + m + 1],
                                         in1=rstd[:], op0=ALU.mult, op1=ALU.mult).then_inc(n_xf, 1)
            for n in range(SEQ // P + 1):
                w = P if n < SEQ // P else SMP
                dve.wait_ge(y_full, 2 * n + 2)
                dve.wait_ge(y_read, 2 * n + 1)
                if n >= 2:
                    dve.wait_ge(y_stored[n % 2], 16 * (n // 2))
                dve.tensor_copy(yrow[n % 2][0:w, 512:DM], pL[0:w, 1, :]).then_inc(y_read, 1)

        @block.tensor
        def _(pe):
            def unit(s, half, a, U, x_hi, x_lo, Xb):
                unit_part(s, half, a, U, x_hi, x_lo, Xb, 0, 8)

            def unit_part(s, half, a, U, x_hi, x_lo, Xb, k0, k1):
                if k0 == 0:
                    pe.wait_ge(acc_free, U + 1)
                for k in range(k0, k1):
                    pe.wait_ge(x_ready, Xb + k + 1)
                    for n, (w, x) in enumerate(((whi, x_hi), (whi, x_lo), (wlo, x_hi))):
                        for hf in range(2):
                            last = pe.matmul(acc[a][:, hf, 0:HALF], w[s][:, k, half * P:(half + 1) * P],
                                             x[:, k, hf * HALF:(hf + 1) * HALF], start=(k == 0 and n == 0),
                                             stop=(k == 7 and n == 2))
                if k1 == 8:
                    last.then_inc(unit_done, 1)

            def panel(s, Pn, U, x_hi, x_lo, Xb):
                pe.wait_ge(lo_done, Pn + 1)
                for a in range(2):
                    unit(s, a, a, U + a, x_hi, x_lo, Xb)

            def square(Ub, x_hi, x_lo, Xb):
                with pe.Fori(0, 2) as i:
                    for s in range(2):
                        panel(s, Ub // 2 + 2 * i + s, Ub + 4 * i + 2 * s, x_hi, x_lo, Xb)

            pe.wait_ge(pool_const, 1)
            pe.wait_ge(vec_landed, 96)
            pe.transpose(pO[:, 0:72], vec_rows[:], ident[0:72, 0:72])
            pe.wait_ge(bias_landed, 16)
            pe.matmul(pO[:, 72:72 + H_B], ones[0:1, :], bias_row[:], start=True, stop=True).then_inc(vec_T, 1)
            pe.wait_ge(x_landed, 32)
            for m in range(NB):
                if m >= 2:
                    pe.wait_ge(xT_read, m - 1)
                for c in range(NCH):
                    last = pe.transpose(pL[:, m % 2, c * P:(c + 1) * P], x_rows[:, c, m * P:(m + 1) * P], ident[:])
                last.then_inc(xT_full, 1)
            for m in range(NB):
                last = pe.transpose(pM[:, m * SMP:(m + 1) * SMP], xs_rows[:, m * P:(m + 1) * P], ident[0:SMP, 0:SMP])
            last.then_inc(xT_full, 1)

            def norm_sum(call):
                pe.wait_ge(n_tot, (NB - 1) * (call + 1))
                for hf in range(2):
                    last = pe.matmul(pL[:, hf, 0:HALF], ones[:], nrm[:, 0, hf * HALF:(hf + 1) * HALF],
                                     start=True, stop=True)
                last.then_inc(n_sum, 1)

            pe.wait_ge(xT_read, NB)
            norm_sum(0)

            def head_products(h):
                Lb = 14 * h
                n_lv = len(LEVELS)

                def chunks(t, c):
                    return t[:, c * CH:(c + 1) * CH]

                if not isinstance(h, int) or h:
                    pe.wait_ge(L_free, Lb)
                pe.wait_ge(acc_free, 4 * h + 5)
                for c in range(NCH):
                    last = pe.transpose(pL[:, 0, c * P:(c + 1) * P], chunks(vT, c), ident[:])
                last.then_inc(L_full, 1)
                pe.wait_ge(prep_dve, 4 * h + 4)
                if not isinstance(h, int) or h:
                    pe.wait_ge(M_free, 3 * h)
                for c in range(NCH):
                    last = pe.transpose(pL[:, 1, c * P:(c + 1) * P], chunks(kh, c), ident[:])
                last.then_inc(L_full, 1)
                pe.transpose(pM[0:SMP, 0:P], vT[:, SEQ:T], ident[:])
                pe.transpose(pM[0:SMP, P:2 * P], kh[:, SEQ:T], ident[:]).then_inc(M_full, 1)
                for n in range(n_lv + 1):
                    b = n % 2
                    pe.wait_ge(L_free, Lb + n + 1)
                    if n < n_lv:
                        pe.wait_ge(lev_X, 2 * n_lv * h + 2 * n + 2)
                        lhs, rhs = X[n], X[n]
                    else:
                        lhs, rhs = None, dg
                    if n >= n_lv - SMP_LEVELS:
                        k = n - (n_lv - SMP_LEVELS)
                        last = pe.matmul(pM[0:SMP, 2 * P + k * SMP:2 * P + (k + 1) * SMP],
                                         lhs[:, SEQ:T] if lhs is not None else ones[:, 0:SMP], rhs[:, SEQ:T],
                                         start=True, stop=True)
                        if n == n_lv:
                            last.then_inc(M_full, 1)
                    for c in range(NCH):
                        last = pe.matmul(pL[:, b, c * P:(c + 1) * P], chunks(lhs, c) if lhs is not None else ones[:],
                                         chunks(rhs, c), start=True, stop=True)
                    last.then_inc(L_full, 1)
                pe.wait_ge(L_free, Lb + 9)
                for c in range(NCH):
                    last = pe.matmul(pL[:, 0, c * P:(c + 1) * P], VK[:, 1, c, :], VK[:, 0, c, :], start=True, stop=True)
                last.then_inc(L_full, 1)
                pe.wait_ge(vblk_ready, h + 1)
                for n in range(2):
                    pe.wait_ge(L_free, Lb + 10 + n)
                    pe.matmul(pL[:, (n + 1) % 2, :], VK[0:SMP, 1, NCH, :],
                              Vblk[:, 4 * n:4 * n + 4, :].rearrange("p s v -> p (s v)"), start=True, stop=True
                              ).then_inc(L_full, 1)
                pe.wait_ge(L_free, Lb + 11)
                if not isinstance(h, int) or h:
                    pe.wait_ge(o_norm, h)
                for c in range(NCH):
                    last = pe.matmul(pO[:, c * P:(c + 1) * P], VK[:, 0, c, :], Amat[:, c, :], start=True, stop=(c == 0))
                    if c:
                        last = pe.matmul(pO[:, c * P:(c + 1) * P], S[:, c - 1, :], chunks(qe, c), start=False, stop=True)
                last.then_inc(o_full, 1)
                pe.wait_ge(M_free, 3 * h + 2)
                pe.wait_ge(s0_landed, 16 * h + 16)
                pe.matmul(pM[:, 0:SMP], VK[0:SMP, 0, NCH, :], As[:], start=True, stop=False)
                for s in range(NSEQ):
                    last = pe.matmul(pM[:, s * NEW:(s + 1) * NEW], S0[:, s, :], qe[:, SEQ + s * NEW:SEQ + (s + 1) * NEW],
                                     start=False, stop=(s == NSEQ - 1))
                last.then_inc(M_full, 1)
                pe.wait_ge(o_sq, 2 * h + 1)
                pe.wait_ge(L_free, Lb + 12)
                pe.matmul(pL[:, 1, :], ones[:], t1[:, 0:SEQ], start=True, stop=True).then_inc(L_full, 1)
                pe.wait_ge(o_sq, 2 * h + 2)
                pe.matmul(pM[:, SMP:2 * SMP], ones[:], t1[:, SEQ:T], start=True, stop=True).then_inc(M_full, 1)

            panel(0, 0, 0, xa_hi, xa_lo, X_N0)
            panel(1, 1, 2, xa_hi, xa_lo, X_N0)
            panel(0, 2, 4, xa_hi, xa_lo, X_N0)
            head_products(0)
            panel(1, 3, 6, xa_hi, xa_lo, X_N0)
            with pe.Fori(2, NB) as h:
                panel(0, 2 * h, 4 * h, xa_hi, xa_lo, X_N0)
                head_products(h - 1)
                panel(1, 2 * h + 1, 4 * h + 2, xa_hi, xa_lo, X_N0)
            head_products(NB - 1)
            square(U_OUT, xa_hi, xa_lo, X_HG)

            def mlp(Ub, Xn, X0, x_hi, x_lo, h_hi, h_lo):
                with pe.Fori(0, FCH) as c:
                    with pe.Fori(0, 2) as i:
                        for s in range(2):
                            panel(s, Ub // 2 + 8 * c + 2 * i + s, Ub + 16 * c + 4 * i + 2 * s, x_hi, x_lo, Xn)
                    with pe.Fori(0, 2) as i:
                        for s in range(2):
                            panel(s, Ub // 2 + 4 + 8 * c + 2 * i + s, Ub + 8 + 16 * c + 4 * i + 2 * s, h_hi, h_lo,
                                  X0 + NB * c)

            norm_sum(n_norm["mlp0"])
            mlp(U_MLP0, X_N1, X_HID0, xa_hi, xa_lo, xb_hi, xb_lo)
            norm_sum(n_norm["mix1"])
            square(U_Q, xa_hi, xa_lo, X_Q)

            def logits(j, n):
                hh, g = divmod(n, 3)
                rows = slice(64 * hh, 64 * hh + 64)
                pe.wait_ge(B_free, 8 * j + n + 3)
                if n == 0:
                    pe.wait_ge(kq_lo, 2 * j + 2)
                for kb, c0 in GROUPS[g]:
                    w = SEQ - kb * P
                    for m, (k, q) in enumerate(((khi, qhi), (khi, qlo), (klo, qhi))):
                        pe.matmul(pL[:, n % 2, c0:c0 + w], k[rows, kb * P:(kb + 1) * P], q[rows, kb * P:SEQ],
                                  start=(m == 0), stop=False)
                    last = pe.matmul(pL[:, n % 2, c0:c0 + P], ident_r[:], neg_r[:], start=False, stop=True)
                last.then_inc(B_full, 1)

            def later_sums(j, n):
                hh, g = divmod(n, 3)
                pe.wait_ge(la_done, 6 * j + n + 1)
                if n == 0:
                    pe.wait_ge(R_free, j + 1)
                pe.wait_ge(u_lo, 6 * j + n + 1)
                for kb, c0 in GROUPS[g]:
                    for k2 in range(kb, NCH):
                        w = SEQ - k2 * P
                        c = c0 + (k2 - kb) * P
                        for u in (uh[hh], ul[hh]):
                            last = pe.matmul(pM[:, c:c + w], (tri_r if k2 == kb else ones_r)[:],
                                             u[:, UOFF[k2]:UOFF[k2] + w], start=(k2 == kb and u is uh[hh]),
                                             stop=(k2 == NCH - 1 and u is ul[hh]))
                last.then_inc(R_full, 1)

            def weighted(j, hh):
                pe.wait_ge(AV_free, 2 * j + hh + 1)
                pe.wait_ge(a_done, 6 * j + 3 * hh + 5)
                for kb in range(NCH):
                    w = SEQ - kb * P
                    last = pe.matmul(pO[:, kb * P:SEQ], vr[:, kb, :], Am[:, UOFF[kb]:UOFF[kb] + w], start=(kb == 0),
                                     stop=(kb == NCH - 1))
                last.then_inc(AV_full, 1)

            def pair(j, par, nxt):
                s = 1 - par
                U = U_KV + 2 * j
                for n, t in enumerate((kf, vf)):
                    if n == 1:
                        pe.wait_ge(la_done, 6 * j + 1)
                    pe.wait_ge(acc_free, U + n + 3)
                    pe.wait_ge(B_free, 8 * j + n + 1)
                    for c in range(NCH):
                        last = pe.transpose(pL[:, n, c * P:(c + 1) * P], t[:, c * P:(c + 1) * P], ident[:])
                    last.then_inc(B_full, 1)
                pe.transpose(pM[0:SMP, 0:P], kf[:, SEQ:T], ident[:])
                pe.transpose(pM[0:SMP, P:2 * P], vf[:, SEQ:T], ident[:]).then_inc(R_full, 1)

                def fill(a, k0, k1):
                    if nxt:
                        if a == 0 and k0 == 0:
                            pe.wait_ge(lo_done, U_KV // 2 + j + 2)
                        unit_part(s, a, a, U + 2 + a, xb_hi, xb_lo, X_KV, k0, k1)

                logits(j, 0)
                logits(j, 1)
                fill(0, 0, 3)
                later_sums(j, 0)
                logits(j, 2)
                fill(0, 3, 6)
                later_sums(j, 1)
                logits(j, 3)
                fill(0, 6, 8)
                later_sums(j, 2)
                logits(j, 4)
                fill(1, 0, 3)
                weighted(j, 0)
                later_sums(j, 3)
                logits(j, 5)
                fill(1, 3, 6)
                later_sums(j, 4)
                fill(1, 6, 8)
                later_sums(j, 5)
                weighted(j, 1)

            panel(0, U_KV // 2, U_KV, xb_hi, xb_lo, X_KV)
            with pe.Fori(0, NPAIR // 2 - 1) as i:
                for par in range(2):
                    pair(2 * i + par, par, True)
            pair(NPAIR - 2, 0, True)
            pair(NPAIR - 1, 1, False)

            pe.wait_ge(la_done, 6 * NPAIR + 1)
            pe.wait_ge(kts_done, NPAIR)
            for h in range(H_B):
                rows = slice(64 * (h % 2), 64 * (h % 2) + 64)
                last = pe.matmul(pL[0:SMP, h % 2, (h // 2) * SMP:(h // 2 + 1) * SMP], kTs[rows, h // 2, :],
                                 qT[rows, h // 2, SEQ:T], start=True, stop=True)
            last.then_inc(new_full, 1)
            pe.wait_ge(new_dve, 4)
            pe.wait_ge(new_chain, 3 + NSEQ)
            for s in range(NSEQ):
                pe.matmul(pM[:, s:s + 1], tlNs[:, s, :], ones[0:SMP, 0:1], start=True, stop=True)
            for n in range(2):
                for u in (uhN, ulN):
                    last = pe.matmul(pL[:, n, :], tri_r[0:SMP, :], u[:, 8 * n:8 * n + 8, :].rearrange(
                        "p h t -> p (h t)"), start=(u is uhN), stop=(u is ulN))
            last.then_inc(new_full, 1)

            def t_fill(s, b, f, nth):
                if f == 0:
                    pe.wait_ge(kp_landed[b], 64 * nth)
                free = (Ta_free, Td_free)[f % 2]
                if f >= 4:
                    pe.wait_ge(free, 4 * s + (f - 4) // 2 + 1)
                elif not isinstance(s, int) or s:
                    pe.wait_ge(free, 4 * s + f // 2 - 1)
                for p in range(4):
                    j = 4 * (f % 2) + p
                    last = pe.transpose(T_bank(f)[:, p * P:(p + 1) * P], Kp[b][:, f // 2, j * P:(j + 1) * P], ident[:])
                last.then_inc(T_full, 1)

            def finish(s):
                pe.wait_ge(O_dve, 2 * s + 2)
                pe.transpose(pM[:, 0:P], Oc[:], ident[:]).then_inc(fin_full, 1)

            def seq(s, b, first, nth, nxt):
                pe.wait_ge(Ta_free, 4 * s + 4)
                pe.wait_ge(Td_free, 4 * s + 4)
                pe.wait_ge(QB_ready, 2 * s + 2)
                for j in range(NPAIR):
                    last = pe.matmul(pM[:], QB[b][:].rearrange("p j c -> p (j c)")[:, j * P:(j + 1) * P],
                                     KT[:, j].rearrange("p g k -> p (g k)"), start=(j == 0), stop=(j == NPAIR - 1))
                last.then_inc(zS_full, 1)
                if nxt:
                    for f in range(8):
                        t_fill(s + 1, 1 - b, f, nth + b)
                pe.wait_ge(zS_act, 4 * s + 4)
                for g in range(NPG):
                    last = pe.transpose(pO[:, g * P:(g + 1) * P], AS[:, g * P:(g + 1) * P], ident[:])
                last.then_inc(AT_full, 1)
                if not first:
                    finish(s - 1)
                pe.wait_ge(vp_landed[b], 64 * nth)
                pe.wait_ge(ANs_ready, s + 1)
                pe.wait_ge(zS_dve, 5 * s + 5)
                for n in range(2):
                    for g in range(NPG):
                        pe.matmul(acc[1][:, n, :], AT[:, g, :], Vp[b][:, g, n * 512:(n + 1) * 512], start=(g == 0),
                                  stop=False)
                    last = pe.matmul(acc[1][:, n, :], ANs[b][:], kvn[:, 1, 4 * n:4 * n + 4, :].rearrange(
                        "p j f -> p (j f)"), start=False, stop=True)
                last.then_inc(O_full, 1)
                if not first:
                    pe.wait_ge(fin_free, 2 * s)

            pe.wait_ge(new_dve, 5)
            pe.wait_ge(new_act, 5)
            for f in range(8):
                t_fill(0, 0, f, 1)
            seq(0, 0, True, 1, True)
            with pe.Fori(0, NSEQ // 2 - 1) as i:
                seq(2 * i + 1, 1, False, i + 1, True)
                seq(2 * i + 2, 0, False, i + 2, True)
            seq(NSEQ - 1, 1, False, NSEQ // 2, False)
            finish(NSEQ - 1)
            square(U_OB, xb_hi, xb_lo, X_OB)
            norm_sum(n_norm["mlp1"])
            mlp(U_MLP1, X_N3, X_HID1, xa_hi, xa_lo, xb_hi, xb_lo)
            norm_sum(n_norm["final"])
            for n in range(SEQ // P + 1):
                w = P if n < SEQ // P else SMP
                for hf in range(2):
                    pe.wait_ge(n_xf, NB * n_app["final"] + 4 * hf + 4)
                    if n:
                        pe.wait_ge(y_read, 2 * n - 1 + hf)
                    for m in range(4):
                        last = pe.transpose(pL[0:w, hf, m * P:(m + 1) * P], nrm[:, 4 * hf + m, n * P:n * P + w], ident[:])
                    last.then_inc(y_full, 1)


_INS = ["x_prompt", "x_sample", "state_hgrn", "cache_k", "cache_v", "page_table", "lb_logits", "w_in_a", "g_onorm_a",
        "w_out_a", "w_kv", "g_kv", "w_q_b", "w_out_b", "sb_bias", "w_up", "w_down", "g_mix", "g_mlp", "g_final"]
_OUTS = [(1, SEQ, DM), (NSEQ, NEW, DM), (1, 1, NB, P, P), (1, NSEQ, NB, P, P), (1, SEQ, H_B, HD), (1, SEQ, H_B, HD),
         (NSEQ, NEW, H_B, HD), (NSEQ, NEW, H_B, HD)]


def kernel(**inputs):
    import numpy as _np
    import concourse.bacc as _bacc
    from concourse import mybir as _mybir
    from concourse.bass_utils import run_bass_kernel_spmd as _run

    nc = _bacc.Bacc("TRN2", target_bir_lowering=False, num_devices=1)
    arrays, args = {}, []
    for name in _INS:
        a = _np.ascontiguousarray(inputs[name])
        arrays[f"in_{name}_dram"] = a
        args.append(nc.dram_tensor(f"in_{name}_dram", a.shape, _mybir.dt.from_np(a.dtype), kind="ExternalInput").ap())
    for i, shape in enumerate(_OUTS):
        args.append(nc.dram_tensor(f"out_{i}_dram", shape, F32, kind="ExternalOutput").ap())
    yoco_step(nc, *args)
    r = _run(nc, [arrays], core_ids=[0])
    return tuple(r.results[0][f"out_{i}_dram"] for i in range(len(_OUTS)))
```
